# Optimizing a Trainium2 kernel written in Bass

```python
import math
import jax, jax.numpy as jnp
from jax import lax
import numpy as np

D_MODEL = 1024
BATCH = 1
SEQ = 512
DEPTH = 2

GRID_W = 64
N_FGROUPS = 4
FGROUP_DIM = 128
F_WIDTH = N_FGROUPS * FGROUP_DIM
N_HEADS = 8
N_KV_HEADS = 2
HEAD_DIM = 64
Q_GROUP = N_HEADS // N_KV_HEADS
Q_WIDTH = N_HEADS * HEAD_DIM
KV_WIDTH = N_KV_HEADS * HEAD_DIM
Q_BLOCK = 128
ROPE_THETA = 10000.0
ROPE_PAIRS = HEAD_DIM // 4
EVEN_IN_WIDTH = F_WIDTH + Q_WIDTH + 2 * KV_WIDTH
EVEN_MIX_WIDTH = F_WIDTH + Q_WIDTH
CHUNK = 128
N_CGROUPS = 8
CGROUP_DIM = D_MODEL // N_CGROUPS
C_WIDTH = N_CGROUPS * CGROUP_DIM
N_EXPERTS = 64
EXPERT_DIM = 256
TOP_K = 8
N_EXPERT_GROUPS = 8
TOPK_GROUPS = 4
ROUTE_SCALE = 2.5
EXPERT_BLOCK = 128
LN_EPS = 1e-5
QK_EPS = 1e-6
DEEPNORM_ALPHA = (2 * DEPTH) ** 0.25
DEEPNORM_BETA = (8 * DEPTH) ** -0.25

kernel_name = "hybrid_fourier_gqa_gmlp_moe_encoder"

def layer_norm(x, g, b):
    xf = x.astype(jnp.float32)
    mu = jnp.mean(xf, axis=-1, keepdims=True)
    var = jnp.mean(jnp.square(xf - mu), axis=-1, keepdims=True)
    y = (xf - mu) * lax.rsqrt(var + LN_EPS)
    return (y * g.astype(jnp.float32) + b.astype(jnp.float32)).astype(x.dtype)

def axial_rope_tables(seq_len):
    rows = seq_len // GRID_W
    row = jnp.repeat(jnp.arange(rows, dtype=jnp.float32), GRID_W)
    col = jnp.tile(jnp.arange(GRID_W, dtype=jnp.float32), rows)
    inv = ROPE_THETA ** (-jnp.arange(ROPE_PAIRS, dtype=jnp.float32) / ROPE_PAIRS)
    ang = jnp.stack([row, col], axis=-1)[:, :, None] * inv
    return jnp.cos(ang), jnp.sin(ang)

def qk_norm_rope(x, gain, cos, sin):
    B, S, H, D = x.shape
    xf = x.astype(jnp.float32)
    xf = xf * lax.rsqrt(jnp.mean(jnp.square(xf), axis=-1, keepdims=True) + QK_EPS)
    xf = (xf * gain.astype(jnp.float32)).reshape(B, S, H, 2, 2, ROPE_PAIRS)
    x1, x2 = xf[..., 0, :], xf[..., 1, :]
    c, s = cos[None, :, None], sin[None, :, None]
    out = jnp.stack([x1 * c - x2 * s, x2 * c + x1 * s], axis=-2)
    return out.reshape(B, S, H, D).astype(x.dtype)

def block_gqa_attention(q, k, v):
    B, S, H, D = q.shape
    n_blocks = S // Q_BLOCK
    qb = q.reshape(B, n_blocks, Q_BLOCK, N_KV_HEADS, Q_GROUP, D).transpose(1, 0, 3, 4, 2, 5)
    scale = 1.0 / math.sqrt(HEAD_DIM)

    def one_block(qblk):
        s = jnp.einsum('bkgqd,bskd->bkgqs', qblk, k, preferred_element_type=jnp.float32) * scale
        p = jax.nn.softmax(s, axis=-1).astype(v.dtype)
        return jnp.einsum('bkgqs,bskd->bqkgd', p, v)

    o = lax.map(one_block, qb)
    return o.transpose(1, 0, 2, 3, 4, 5).reshape(B, S, H * D)

def fourier_attention_mixer(x, w_in, w_fourier, q_gain, k_gain, w_out, cos, sin):
    B, S, _ = x.shape
    h = x @ w_in
    a, q, k, v = jnp.split(h, [F_WIDTH, F_WIDTH + Q_WIDTH, F_WIDTH + Q_WIDTH + KV_WIDTH], axis=-1)
    a = a.reshape(B, S, N_FGROUPS, FGROUP_DIM).astype(jnp.float32)
    af = jnp.fft.fft2(a, axes=(1, 3), norm='ortho').real.astype(x.dtype)
    a_out = jnp.einsum('bsgc,gcd->bsgd', af, w_fourier).reshape(B, S, F_WIDTH)
    q = qk_norm_rope(q.reshape(B, S, N_HEADS, HEAD_DIM), q_gain, cos, sin)
    k = qk_norm_rope(k.reshape(B, S, N_KV_HEADS, HEAD_DIM), k_gain, cos, sin)
    v = v.reshape(B, S, N_KV_HEADS, HEAD_DIM)
    attn = block_gqa_attention(q, k, v)
    return jnp.concatenate([a_out, attn], axis=-1) @ w_out

def spatial_gating_mixer(x, w_in, b_in, v_g, v_b, w_s, b_s, w_out):
    B, S, _ = x.shape
    h = jax.nn.gelu(x @ w_in + b_in, approximate=False)
    u, v = jnp.split(h, 2, axis=-1)
    v = layer_norm(v, v_g, v_b).reshape(B, S // CHUNK, CHUNK, N_CGROUPS, CGROUP_DIM)
    v = jnp.einsum('gpq,bnqgc->bnpgc', w_s, v) + b_s.T[:, :, None]
    return (u * v.reshape(B, S, C_WIDTH)) @ w_out

def moe_ffn(x, router_w, router_b, w_gate, w_up, w_down, sh_gate, sh_up, sh_down):
    B, S, D = x.shape
    T = B * S
    xt = x.reshape(T, D)
    scores = jax.nn.sigmoid((xt @ router_w).astype(jnp.float32))
    sel = scores + router_b.astype(jnp.float32)
    gsc = lax.top_k(sel.reshape(T, N_EXPERT_GROUPS, N_EXPERTS // N_EXPERT_GROUPS), 2)[0].sum(-1)
    _, gidx = lax.top_k(gsc, TOPK_GROUPS)
    gmask = jnp.any(gidx[..., None] == jnp.arange(N_EXPERT_GROUPS), axis=1)
    emask = jnp.repeat(gmask, N_EXPERTS // N_EXPERT_GROUPS, axis=1)
    _, eidx = lax.top_k(jnp.where(emask, sel, -jnp.inf), TOP_K)
    wts = jnp.take_along_axis(scores, eidx, axis=1)
    wts = wts / jnp.sum(wts, axis=-1, keepdims=True) * ROUTE_SCALE

    A = T * TOP_K
    e_flat = eidx.reshape(A)
    tok_flat = jnp.arange(A, dtype=jnp.int32) // TOP_K
    w_flat = wts.reshape(A)
    order = jnp.argsort(e_flat)
    e_sorted = e_flat[order]
    counts = jnp.bincount(e_flat, length=N_EXPERTS)
    padded = (counts + EXPERT_BLOCK - 1) // EXPERT_BLOCK * EXPERT_BLOCK
    pad_end = jnp.cumsum(padded)
    pad_start = pad_end - padded
    start = jnp.cumsum(counts) - counts
    dest = pad_start[e_sorted] + (jnp.arange(A) - start[e_sorted])
    n_blocks = -(-A // EXPERT_BLOCK) + N_EXPERTS
    P = n_blocks * EXPERT_BLOCK
    row_tok = jnp.full((P,), T, jnp.int32).at[dest].set(tok_flat[order])
    row_w = jnp.zeros((P,), jnp.float32).at[dest].set(w_flat[order])
    blk_e = jnp.minimum(jnp.searchsorted(pad_end, jnp.arange(n_blocks) * EXPERT_BLOCK, side='right'),
                        N_EXPERTS - 1)
    x_pad = jnp.concatenate([xt, jnp.zeros((1, D), xt.dtype)], axis=0)

    def expert_block(args):
        toks, rw, e = args
        xb = x_pad[toks]
        hb = jax.nn.silu(xb @ w_gate[e]) * (xb @ w_up[e])
        return (hb @ w_down[e]) * rw[:, None].astype(xb.dtype)

    yb = lax.map(expert_block, (row_tok.reshape(n_blocks, EXPERT_BLOCK),
                                row_w.reshape(n_blocks, EXPERT_BLOCK), blk_e))
    routed = jax.ops.segment_sum(yb.reshape(P, D), row_tok, num_segments=T + 1)[:T]
    shared = (jax.nn.silu(xt @ sh_gate) * (xt @ sh_up)) @ sh_down
    return (routed + shared).reshape(B, S, D)

def setup_inputs(seed: int = 0) -> dict:
    key = jax.random.key(seed)
    ks = jax.random.split(key, 32)
    f32 = jnp.float32
    ne, no = (DEPTH + 1) // 2, DEPTH // 2

    def nrm(k, shape, scale):
        return jax.random.normal(k, shape, f32) * scale

    return {
        "x": nrm(ks[0], (BATCH, SEQ, D_MODEL), 1.0),
        "ln_in_g": 1.0 + nrm(ks[1], (D_MODEL,), 0.05),
        "ln_in_b": nrm(ks[2], (D_MODEL,), 0.02),
        "e_w_in": nrm(ks[3], (ne, D_MODEL, EVEN_IN_WIDTH), D_MODEL ** -0.5),
        "e_w_fourier": nrm(ks[4], (ne, N_FGROUPS, FGROUP_DIM, FGROUP_DIM), FGROUP_DIM ** -0.5),
        "e_q_gain": 1.0 + nrm(ks[5], (ne, HEAD_DIM), 0.1),
        "e_k_gain": 1.0 + nrm(ks[6], (ne, HEAD_DIM), 0.1),
        "e_w_out": nrm(ks[7], (ne, EVEN_MIX_WIDTH, D_MODEL), EVEN_MIX_WIDTH ** -0.5 * DEEPNORM_BETA),
        "o_w_in": nrm(ks[8], (no, D_MODEL, 2 * C_WIDTH), D_MODEL ** -0.5),
        "o_b_in": nrm(ks[9], (no, 2 * C_WIDTH), 0.02),
        "o_v_ln_g": 1.0 + nrm(ks[10], (no, C_WIDTH), 0.05),
        "o_v_ln_b": nrm(ks[11], (no, C_WIDTH), 0.02),
        "o_w_spatial": nrm(ks[12], (no, N_CGROUPS, CHUNK, CHUNK), CHUNK ** -0.5),
        "o_b_spatial": 1.0 + nrm(ks[13], (no, N_CGROUPS, CHUNK), 0.1),
        "o_w_out": nrm(ks[14], (no, C_WIDTH, D_MODEL), C_WIDTH ** -0.5 * DEEPNORM_BETA),
        "ln_mix_g": 1.0 + nrm(ks[15], (DEPTH, D_MODEL), 0.05),
        "ln_mix_b": nrm(ks[16], (DEPTH, D_MODEL), 0.02),
        "ln_ffn_g": 1.0 + nrm(ks[17], (DEPTH, D_MODEL), 0.05),
        "ln_ffn_b": nrm(ks[18], (DEPTH, D_MODEL), 0.02),
        "router_w": nrm(ks[19], (DEPTH, D_MODEL, N_EXPERTS), D_MODEL ** -0.5),
        "router_b": nrm(ks[20], (DEPTH, N_EXPERTS), 0.01),
        "exp_w_gate": nrm(ks[21], (DEPTH, N_EXPERTS, D_MODEL, EXPERT_DIM), D_MODEL ** -0.5),
        "exp_w_up": nrm(ks[22], (DEPTH, N_EXPERTS, D_MODEL, EXPERT_DIM), D_MODEL ** -0.5),
        "exp_w_down": nrm(ks[23], (DEPTH, N_EXPERTS, EXPERT_DIM, D_MODEL), EXPERT_DIM ** -0.5 * DEEPNORM_BETA),
        "sh_w_gate": nrm(ks[24], (DEPTH, D_MODEL, EXPERT_DIM), D_MODEL ** -0.5),
        "sh_w_up": nrm(ks[25], (DEPTH, D_MODEL, EXPERT_DIM), D_MODEL ** -0.5),
        "sh_w_down": nrm(ks[26], (DEPTH, EXPERT_DIM, D_MODEL), EXPERT_DIM ** -0.5 * DEEPNORM_BETA),
    }

def reference(x, ln_in_g, ln_in_b, e_w_in, e_w_fourier, e_q_gain, e_k_gain, e_w_out,
              o_w_in, o_b_in, o_v_ln_g, o_v_ln_b, o_w_spatial, o_b_spatial, o_w_out,
              ln_mix_g, ln_mix_b, ln_ffn_g, ln_ffn_b, router_w, router_b,
              exp_w_gate, exp_w_up, exp_w_down, sh_w_gate, sh_w_up, sh_w_down):
    x = layer_norm(x, ln_in_g, ln_in_b)
    cos, sin = axial_rope_tables(x.shape[1])
    for i in range(DEPTH):
        j = i // 2
        if i % 2 == 0:
            mix = fourier_attention_mixer(x, e_w_in[j], e_w_fourier[j], e_q_gain[j], e_k_gain[j],
                                          e_w_out[j], cos, sin)
        else:
            mix = spatial_gating_mixer(x, o_w_in[j], o_b_in[j], o_v_ln_g[j], o_v_ln_b[j],
                                       o_w_spatial[j], o_b_spatial[j], o_w_out[j])
        x = layer_norm(DEEPNORM_ALPHA * x + mix, ln_mix_g[i], ln_mix_b[i])
        ffn = moe_ffn(x, router_w[i], router_b[i], exp_w_gate[i], exp_w_up[i], exp_w_down[i],
                      sh_w_gate[i], sh_w_up[i], sh_w_down[i])
        x = layer_norm(DEEPNORM_ALPHA * x + ffn, ln_ffn_g[i], ln_ffn_b[i])
    return x


_drawn_inputs = setup_inputs


def setup_inputs(seed=0):
    import zlib

    import numpy as np

    out = dict(_drawn_inputs(seed))
    spreads = {}
    factors = {'e_q_gain': 4.102, 'e_k_gain': 3.533, 'o_b_in': 2.716, 'o_v_ln_b': 3.634}
    for name, (base, spread) in spreads.items():
        noise = np.random.default_rng([zlib.crc32(name.encode()), seed]).standard_normal(out[name].shape)
        drawn = base * np.exp(spread * noise) if base else spread * noise
        out[name] = __import__('jax').numpy.asarray(drawn.astype(out[name].dtype))
    for name, factor in factors.items():
        out[name] = (out[name] * factor).astype(out[name].dtype)
    return out
```

```python
import math

import numpy as np

import concourse.bass as bass
from concourse import mybir
from contextlib import ExitStack

F32 = mybir.dt.float32
BF16 = mybir.dt.bfloat16
I32 = mybir.dt.int32
ALU = mybir.AluOpType
ACT = mybir.ActivationFunctionType
AX = mybir.AxisListType.X

P = 128
D = 1024
T = 512
NT = T // P
NK = D // P
GRID_W = 64
N_FGROUPS = 4
N_HEADS = 8
HEAD_DIM = 64
PAIRS = N_HEADS // 2
F_WIDTH = 512
QKV_WIDTH = 768
QK_HEADS = 10
E_IN = F_WIDTH + QKV_WIDTH
CH = 8
E = 64
FE = 256
FC = FE // P
TOP_K = 8
N_EGROUPS = 8
TOPK_GROUPS = 4
ROUTE_SCALE = 2.5
LN_EPS = 1e-5
QK_EPS = 1e-6
ALPHA = 4.0 ** 0.25
DEPTH = 2

NB = 96
QUADS = E // 4
ROW_STEPS = (NB, 80, 64)
LEVELS = -(-T // NB)
SLOTS = 4
SLOT = 3 * D * FE // P
PER_ITEM = 48
IT_WIN, IT_DFT, IT_WOUT, IT_SH0 = 0, 2, 3, 5
IT_EXP = (6, 6 + E + 7)
IT_OWIN, IT_OWOUT, IT_SH1 = 6 + E, 6 + E + 4, 6 + E + 6
BIG = 1.0e30


def slot_of(item):
    return item % SLOTS


def full_value(item):
    return PER_ITEM * (item // SLOTS + 1)


def build(nc, t, out):
    with ExitStack() as ctx:
        def sb(name, shape, dt=F32):
            return ctx.enter_context(nc.sbuf_tensor(name, shape, dt))

        def sem(name):
            return ctx.enter_context(nc.semaphore(name))

        ring = sb("ring", [P, SLOTS, SLOT])
        xres = sb("xres", [P, NT, D])
        xperm = sb("xperm", [P, NT, D])
        xT = sb("xT", [P, NK, T])
        lnp = sb("lnp", [P, 2, D])
        consts = sb("consts", [P, 128 + 512 + 64 + NB + 2])
        ident = consts[:, 0:128]
        rope_c = consts[:, 128:384].rearrange("p (t d) -> p t d", t=NT)
        rope_s = consts[:, 384:640].rearrange("p (t d) -> p t d", t=NT)
        earlier = consts[:, 640:704].rearrange("p (i j) -> p i j", i=8)
        iota = consts[:, 704:704 + NB]
        negslot = consts[:, 704 + NB:705 + NB]
        dump = consts[:, 705 + NB:706 + NB]
        bconsts = sb("bconsts", [P, 256 + 12], BF16)
        before = bconsts[:, 0:128]
        ones = bconsts[:, 128:256]
        posb = bconsts[:, 256:268].rearrange("p (t c) -> p t c", t=NT)
        zeros = sb("zeros", [P, 256])
        work = sb("work", [P, 13000])

        def carve(*sizes):
            at, got = 0, []
            for n in sizes:
                got.append(work[:, at:at + n])
                at += n
            assert at <= 13000, at
            return got

        stats_w, rest_at = work[:, 0:96], 96
        stats = stats_w[:, 0:48].rearrange("p (t h s) -> p t h s", t=NT, h=2)
        mv = stats_w[:, 48:56].rearrange("p (t s) -> p t s", t=NT)
        vare = stats_w[:, 56:60]
        std = stats_w[:, 60:64]
        rstd = stats_w[:, 64:68]

        _, qkv_w, rot_w, qkT_w, aT_w, fw_w, gain_w, sm_w, tmp_w = carve(
            96, NT * QKV_WIDTH, NT * 640, 5 * T, 4 * T, 1024, 128, 96, 1280)
        qkv = qkv_w.rearrange("p (t c) -> p t c", t=NT)
        rot = rot_w.rearrange("p (t c) -> p t c", t=NT)
        attn = rot_w[:, 0:NT * 512].rearrange("p (t c) -> p t c", t=NT)
        qkT = qkT_w.rearrange("p (i t) -> p i t", i=5)
        aT = aT_w.rearrange("p (g t) -> p g t", g=4)
        probs = aT_w[:, 0:1024].rearrange("p (b k) -> p b k", b=2)
        probsT = aT_w[:, 1024:2048].rearrange("p (b c q) -> p b c q", b=2, c=4)
        fw = fw_w.rearrange("p (g s d) -> p g s d", g=4, s=2)
        tmp1, tmp2 = tmp_w[:, 0:640], tmp_w[:, 640:1280]
        gains = gain_w.rearrange("p (a d) -> p a d", a=2)
        qk_ss, qk_rs = sm_w[:, 0:40], sm_w[:, 40:80]
        nmax, rsum, rinv = sm_w[:, 80:82], sm_w[:, 82:86], sm_w[:, 86:88]
        zmix = xperm[:].rearrange("p t (g s d) -> p t g s d", g=4, s=2)
        catT = xT

        _, uT_w, v_w, ws_w, wsT_w, bv_w, bs_w, bu_w = carve(96, CH * T, NT * D, D, D, D, D, CH)
        uT = uT_w.rearrange("p (g t) -> p g t", g=CH)
        vn = v_w.rearrange("p (t c) -> p t c", t=NT)
        ws = ws_w.rearrange("p (g q) -> p g q", g=CH)
        wsT = wsT_w.rearrange("p (g q) -> p g q", g=CH)
        bs = bs_w.rearrange("p (g q) -> p g q", g=CH)
        bu_col = bu_w
        gate_tmp = ws_w.rearrange("p (b t) -> p b t", b=2)

        router = work[:, 12424:12424 + NK * E].rearrange("p (j e) -> p j e", j=NK)
        rb_w = work[:, 12936:12936 + E]
        (_, sc_w, sel_w, selm_w, rep_w, m8_w, g_w, cmp_w, rank_w, mask_w, tab_w, pe_w, pi_w,
         ix_w, sh_w, xgT_w, sil_w, h_w, y_w) = carve(
            96, NT * E, NT * E, NT * E, NT * E, 256 + 32, 160, 3 * 256, NT * E, NT * E // 2,
            NT * E * 3, 4 * NT * NB // 2, 24 + 8, 4 * E + 16, 2 * D, 2 * NK * NB, 2 * FC * NB, 2 * FC * NB, 2 * D)
        scores, sel, selm, rep = (w.rearrange("p (t e) -> p t e", t=NT) for w in (sc_w, sel_w, selm_w, rep_w))
        m8 = m8_w[:, 0:256].rearrange("p (t g k) -> p t g k", t=NT, g=N_EGROUPS)
        v8 = m8_w[:, 256:288].rearrange("p (t k) -> p t k", t=NT)
        gsc, grank, gmask, gpen = (g_w[:, 32 * i:32 * i + 32].rearrange("p (t g) -> p t g", t=NT) for i in range(4))
        wsum, wfac = g_w[:, 128:132], g_w[:, 132:136]
        cmps = [cmp_w[:, 256 * i:256 * i + 256].rearrange("p (t i j) -> p t i j", t=NT, i=8) for i in range(3)]
        rankm = rank_w.rearrange("p (t e) -> p t e", t=NT)
        maskb = mask_w.bitcast(BF16).rearrange("p (t e) -> p t e", t=NT)
        tab = tab_w.bitcast(BF16).rearrange("p (t e c) -> p t e c", t=NT, e=E)
        pick = pe_w.bitcast(BF16).rearrange("p (b t s) -> p b t s", b=4, t=NT)
        pi = pi_w[:, 0:24].rearrange("p (e c) -> p e c", e=4)
        pi_idx, pi_wt = pi_w[:, 24:28], pi_w[:, 28:32]
        idx_f, w_slot = ix_w[:, 0:E], ix_w[:, E:2 * E]
        idx_tab = ix_w[:, 2 * E:3 * E].bitcast(I32)
        cnt_tab = ix_w[:, 3 * E:4 * E].bitcast(I32)
        cnt_max = ix_w[:, 4 * E:4 * E + 1].bitcast(I32)
        idx_cur = ix_w[:, 4 * E + 4:4 * E + 8].bitcast(I32)
        of_idx = ix_w[:, 4 * E + 8:4 * E + 9].bitcast(I32)
        of_f, of_w1, of_w2, of_wt = (ix_w[:, 4 * E + 9 + i:4 * E + 10 + i] for i in range(4))
        xg = xperm[:]
        xT_w = xT[:].rearrange("p j t -> p (j t)")
        sh_down = xT_w[:, 0:2048].rearrange("p (c d) -> p c d", c=FC)
        xgT = xgT_w.rearrange("p (b j s) -> p b j s", b=2, j=NK)
        sil = sil_w.rearrange("p (b c s) -> p b c s", b=2, c=FC)
        hT = h_w.rearrange("p (b c s) -> p b c s", b=2, c=FC)
        ysb = y_w.rearrange("p (b d) -> p b d", b=2)
        sh_sil = sh_w[:, 0:FC * T].rearrange("p (c t) -> p c t", c=FC)
        sh_h = sh_w[:, FC * T:2 * FC * T].rearrange("p (c t) -> p c t", c=FC)
        of_gate = xT_w[:, 0:2048].rearrange("p (j f) -> p j f", j=NK)
        of_up = xT_w[:, 2048:4096].rearrange("p (j f) -> p j f", j=NK)
        of_down = xperm[:, 2:4, :]

        ps = ctx.enter_context(nc.psum_tensor("ps", [P, 8, 512], F32))

        xs = [nc.dram_tensor(f"tokens{l}", [T, D], F32).ap() for l in range(DEPTH)]
        acc = [nc.dram_tensor(f"sum{l}", [T, D], F32).ap() for l in range(DEPTH)]

        def rings(item, lo, hi):
            return ring[:, slot_of(item), lo:hi]

        def win(j):
            it = IT_WIN + j // 4
            return rings(it, (j % 4) * E_IN, (j % 4 + 1) * E_IN)

        dft_c = rings(IT_DFT, 0, 2048).rearrange("p (t s) -> p t s", t=NT)
        dft_s = rings(IT_DFT, 2048, 4096).rearrange("p (t s) -> p t s", t=NT)
        chn_c = rings(IT_DFT, 4096, 4224)
        chn_s = rings(IT_DFT, 4224, 4352)
        wfour = rings(IT_DFT, 4352, 4864)

        def wout(first, i):
            return rings(first + i // 4, (i % 4) * D, (i % 4 + 1) * D)

        def owin(n):
            return rings(IT_OWIN + n, 0, 4096).rearrange("p (j c) -> p j c", j=NK)

        def expert(slot):
            w = ring[:, slot, :]
            return (w[:, 0:2048].rearrange("p (j f) -> p j f", j=NK),
                    w[:, 2048:4096].rearrange("p (j f) -> p j f", j=NK),
                    w[:, 4096:6144].rearrange("p (c d) -> p c d", c=FC))

        x_in, const_in, bconst_in = [sem(f"x_in{tt}") for tt in range(NT)], sem("const_in"), sem("bconst_in")
        slot_full = [sem(f"slot_full{s}") for s in range(SLOTS)]
        lnp_in, small_in = sem("lnp_in"), sem("small_in")
        ln_stats, ln_std, ln_done = sem("ln_stats"), sem("ln_std"), sem("ln_done")
        perm_done = sem("perm_done")
        tr_done, xT_dve, xT_act = sem("tr_done"), sem("xT_dve"), sem("xT_act")
        dve_step, pool_step = sem("dve_step"), sem("pool_step")
        sp_tick, dve_tick, pool_tick = sem("sp_tick"), sem("dve_tick"), sem("pool_tick")
        aT_mm, aT_cp, qkv_mm, qkv_cp = sem("aT_mm"), sem("aT_cp"), sem("qkv_mm"), sem("qkv_cp")
        fw_mm, fw_cp, z_mm, z_cp = sem("fw_mm"), sem("fw_cp"), sem("z_mm"), sem("z_cp")
        four_mm, four_cp = sem("four_mm"), sem("four_cp")
        qk_ssq, qk_root, rot_done, qkT_tr, qkT_cp = (sem(n) for n in ("qk_ssq", "qk_root", "rot_done", "qkT_tr", "qkT_cp"))
        s_mm, max_done, p_done, pT_tr, pT_cp = (sem(n) for n in ("s_mm", "max_done", "p_done", "pT_tr", "pT_cp"))
        o_mm, rinv_done, o_cp, atT_tr, atT_cp = (sem(n) for n in ("o_mm", "rinv_done", "o_cp", "atT_tr", "atT_cp"))
        wout_mm, resid_done = sem("wout_mm"), sem("resid_done")
        wsT_tr, wsT_cp, v_mm, v_pre, v_act = (sem(n) for n in ("wsT_tr", "wsT_cp", "v_mm", "v_pre", "v_act"))
        vln_stats, vln_std, vln_done = (sem(n) for n in ("vln_stats", "vln_std", "vln_done"))
        u_mm, u_act, sp_mm, uv_done = (sem(n) for n in ("u_mm", "u_act", "sp_mm", "uv_done"))
        xs_out, zero_set, acc_out = sem("xs_out"), sem("zero_set"), sem("acc_out")
        lg_mm, sg_done, mask_done, rk_mm, tab_done, counts_ready = (
            sem(n) for n in ("lg_mm", "sg_done", "mask_done", "rk_mm", "tab_done", "counts_ready"))
        shg_mm, sh_silu, sh_mul, shd_mm, sh_y = (sem(n) for n in ("shg_mm", "sh_silu", "sh_mul", "shd_mm", "sh_y"))
        router_in, sh_down_in = sem("router_in"), sem("sh_down_in")
        pick_done, pick_mm, pi_cp, pi_mid, idx_done, idx_cp = (
            sem(n) for n in ("pick_done", "pick_mm", "pi_cp", "pi_mid", "idx_done", "idx_cp"))
        gathered = [sem(f"gathered{b}") for b in range(4)]
        scattered = [sem(f"scattered{b}") for b in range(2)]
        xg_tr, xgT_dve, xgT_act = sem("xg_tr"), sem("xgT_dve"), sem("xgT_act")
        gate_mm, up_mm, silu_done, h_done = sem("gate_mm"), sem("up_mm"), sem("silu_done"), sem("h_done")
        down_mm, y_dve, y_act = sem("down_mm"), sem("y_dve"), sem("y_act")
        counts_read = sem("counts_read")
        acc_ready, acc_in, acc_sum = sem("acc_ready"), [sem(f"acc_in{tt}") for tt in range(NT)], sem("acc_sum")
        first_sum = sem("first_sum")
        OF = ["of_w", "of_pick", "of_pi", "of_ix", "of_gat", "of_tr", "of_xt", "of_gu", "of_si", "of_h", "of_dn", "of_y", "of_sc", "of_gat_dma", "of_sc_dma", "of_level"]
        of = [{n: sem(f"{n}{l}") for n in OF} for l in range(DEPTH)]
        out_done = sem("out_done")
        block = ctx.enter_context(nc.Block())

        class Steps:

            def __init__(self, eng, s):
                self.eng, self.s, self.n = eng, s, 0

            def done(self, ins):
                self.n += 1
                ins.then_inc(self.s, 1)

            def wait(self):
                self.eng.wait_ge(self.s, self.n)

        def overflow(eng, l, produced, body, level=None):
            s = of[l]
            eng.wait_ge(counts_ready, l + 1)
            most = eng.value_load(cnt_max[0:1, 0:1], min_val=0, max_val=T)
            with eng.If(most > NB):
                with eng.Fori(1, LEVELS) as b:
                    with eng.If(most > b * NB):
                        if level is not None:
                            level(b)
                        with eng.Fori(0, E) as e:
                            count = eng.value_load(cnt_tab[0:1, bass.ds(e, 1)], min_val=0, max_val=T)
                            with eng.If(count > b * NB):
                                body(s, e, b * E + e - E)
                            with eng.Else():
                                eng.drain()
                                for name, by in produced:
                                    eng.sem_inc(s[name], by)
                            eng.nop()
                    eng.nop()
            eng.nop()

        def overflow_sp(sp, l):
            def body(s, e, q):
                with sp.If(q > 0):
                    sp.wait_ge(s["of_sc"], q)
                    sp.sem_inc(sp_tick, 1)
                sp.nop()
                for dst, name in ((of_gate, "exp_w_gate"), (of_up, "exp_w_up")):
                    sp.dma_start(dst, t[name][l, bass.ds(e, 1), :, :].rearrange("a (p j) f -> p (a j) f", j=NK))\
                        .then_inc(s["of_w"], 16)
                sp.dma_start(of_down, t["exp_w_down"][l, bass.ds(e, 1), :, :].rearrange("a (p c) d -> p (a c) d", c=FC))\
                    .then_inc(s["of_w"], 16)
                sp.wait_ge(s["of_w"], q * 48 + 48)
                sp.sem_inc(sp_tick, 1)

            sp.wait_ge(down_mm, (l + 1) * E)
            overflow(sp, l, [("of_w", 48)], body)

        def overflow_pe(pe, l):
            def body(s, e, q):
                pe.wait_ge(s["of_pick"], q + 1)
                for tt in range(NT):
                    ins = mm(ps[0:NB, 7, 0:6], pick[:, 0, tt, :],
                             tab[:, tt, bass.ds(e, 1), :].rearrange("p a c -> p (a c)"), tt == 0, tt == NT - 1)
                ins.then_inc(s["of_pi"], 1)
                pe.wait_ge(s["of_gat"], q + 1)
                for j in range(NK):
                    ins = nc.tensor.transpose(ps[:, j // 4, (j % 4) * NB:(j % 4 + 1) * NB],
                                              xg[0:NB, 0, j * P:(j + 1) * P], ident[0:NB, 0:NB])
                ins.then_inc(s["of_tr"], 1)
                pe.wait_ge(s["of_xt"], q + 1)
                pe.wait_ge(s["of_w"], q * 48 + 48)
                for w, bank in ((of_gate, 2), (of_up, 3)):
                    for c in range(FC):
                        for j in range(NK):
                            ins = mm(ps[:, bank, c * NB:(c + 1) * NB], w[:, j, c::FC], xgT[:, 0, j, :],
                                     j == 0, j == NK - 1)
                ins.then_inc(s["of_gu"], 1)
                pe.wait_ge(s["of_h"], q + 1)
                for hf in range(2):
                    for c in range(FC):
                        ins = mm(ps[0:NB, 4 + hf, :], hT[:, 0, c, :], of_down[:, c, hf * 512:(hf + 1) * 512],
                                 c == 0, c == FC - 1)
                ins.then_inc(s["of_dn"], 1)

            pe.wait_ge(y_dve, (l + 1) * E)
            pe.wait_ge(y_act, (l + 1) * E)
            overflow(pe, l, [("of_pi", 1), ("of_tr", 1), ("of_gu", 1), ("of_dn", 1)], body)

        def overflow_act(act, l):
            def body(s, e, q):
                act.wait_ge(s["of_gu"], q + 1)
                nc.scalar.activation(sil[:, 0, :, :], ps[:, 2, 0:FC * NB].rearrange("p (c s) -> p c s", c=FC), ACT.Silu)\
                    .then_inc(s["of_si"], 1)

            overflow(act, l, [("of_si", 1)], body)

        def overflow_dve(dve, step, l):
            s = of[l]

            def level(b):
                nc.vector.tensor_scalar(rankm, rankm, float(NB), None, ALU.subtract).then_inc(s["of_level"], 1)
                dve.wait_ge(s["of_level"], b)
                dve.sem_inc(dve_tick, 1)

            def body(s, e, q):
                with dve.If(q > 0):
                    dve.wait_ge(s["of_sc"], q)
                    dve.sem_inc(dve_tick, 1)
                dve.nop()
                nc.vector.tensor_tensor(pick[:, 0, :, :], rankm[:, :, bass.ds(e, 1)].to_broadcast([P, NT, NB]),
                                        iota.unsqueeze(1).to_broadcast([P, NT, NB]), ALU.is_equal).then_inc(s["of_pick"], 1)
                dve.wait_ge(s["of_pi"], q + 1)
                nc.vector.tensor_copy(pi_w[0:NB, 0:6], ps[0:NB, 7, 0:6]).then_inc(s["of_ix"], 1)
                dve.wait_ge(s["of_ix"], q * 4 + 1)
                nc.vector.scalar_tensor_tensor(of_f[0:NB, :], pi_w[0:NB, 2:3], negslot[0:NB, :], pi_w[0:NB, 0:1],
                                               ALU.mult, ALU.add)
                nc.vector.tensor_tensor(of_w1[0:NB, :], pi_w[0:NB, 3:4], pi_w[0:NB, 4:5], ALU.add).then_inc(s["of_ix"], 1)
                dve.wait_ge(s["of_ix"], q * 4 + 2)
                nc.vector.tensor_tensor(of_wt[0:NB, :], of_w1[0:NB, :], pi_w[0:NB, 5:6], ALU.add).then_inc(s["of_ix"], 1)
                nc.vector.scalar_tensor_tensor(of_idx[0:NB, :], of_f[0:NB, :], dump[0:NB, :], pi_w[0:NB, 1:2],
                                               ALU.add, ALU.add).then_inc(s["of_ix"], 1)
                dve.wait_ge(s["of_tr"], q + 1)
                nc.vector.tensor_copy(xgT[:, 0, :, :].rearrange("p (a k) s -> p a (k s)", a=2), ps[:, 0:2, 0:4 * NB])\
                    .then_inc(s["of_xt"], 1)
                dve.wait_ge(s["of_si"], q + 1)
                nc.vector.tensor_tensor(hT[:, 0, :, :], sil[:, 0, :, :],
                                        ps[:, 3, 0:FC * NB].rearrange("p (c s) -> p c s", c=FC), ALU.mult)\
                    .then_inc(s["of_h"], 1)
                dve.wait_ge(s["of_dn"], q + 1)
                dve.wait_ge(s["of_ix"], q * 4 + 4)
                nc.vector.tensor_scalar(ysb[0:NB, 0, :], ps[0:NB, 4:6, :].rearrange("p b c -> p (b c)"), of_wt[0:NB, :],
                                        None, ALU.mult).then_inc(s["of_y"], 1)

            for b in range(2):
                dve.wait_ge(scattered[b], 16 * (l + 1) * E // 2)
            dve.wait_ge(y_dve, (l + 1) * E)
            overflow(dve, l, [("of_pick", 1), ("of_ix", 4), ("of_xt", 1), ("of_h", 1), ("of_y", 1)], body, level)

        def overflow_pool(pool, l):
            landed = pool.alloc_register(f"of_landed{l}")
            pool.reg_mov(landed, 0)

            def body(s, e, q):
                pool.reg_add(landed, landed, 16)
                dma_count = pool.snap(landed)
                pool.wait_ge(s["of_ix"], q * 4 + 4)
                pool.sem_inc(pool_tick, 1)
                pool.indirect_dma_start(out=xg[0:NB, 0, :], out_offset=None, in_=xs[l],
                                        in_offset=bass.IndirectOffsetOnAxis(ap=of_idx[0:NB, :], axis=0),
                                        bounds_check=T - 1, oob_is_err=False).then_inc(s["of_gat_dma"], 16)
                pool.wait_ge(s["of_gat_dma"], dma_count)
                pool.sem_inc(s["of_gat"], 1)
                pool.wait_ge(s["of_y"], q + 1)
                pool.sem_inc(pool_tick, 1)
                pool.indirect_dma_start(out=acc[l], out_offset=bass.IndirectOffsetOnAxis(ap=of_idx[0:NB, :], axis=0),
                                        in_=ysb[0:NB, 0, :], in_offset=None, bounds_check=T - 1, oob_is_err=False,
                                        compute_op=ALU.add).then_inc(s["of_sc_dma"], 16)
                pool.wait_ge(s["of_sc_dma"], dma_count)
                pool.sem_inc(s["of_sc"], 1)

            overflow(pool, l, [("of_gat", 1), ("of_sc", 1)], body)

        @block.sync
        def _(sp):
            def load3(item, parts):
                s = slot_full[slot_of(item)]
                for dst, src in parts:
                    sp.dma_start(dst, src).then_inc(s, 16)

            for tt in range(NT):
                sp.dma_start(xres[:, tt, :], t["x"][0, tt * P:(tt + 1) * P, :]).then_inc(x_in[tt], 16)
                if tt == 0:
                    for a, name in enumerate(("ln_in_g", "ln_in_b")):
                        sp.dma_start(lnp[:, a, :], t[name].partition_broadcast(P)).then_inc(lnp_in, 16)
            w = t["e_w_in"][0].rearrange("(p j) c -> p j c", j=NK)
            for it in range(2):
                load3(IT_WIN + it, [(rings(IT_WIN + it, a * E_IN, b * E_IN).rearrange("p (j c) -> p j c", c=E_IN),
                                     w[:, 4 * it + a:4 * it + b, :]) for a, b in ((0, 2), (2, 3), (3, 4))])
            load3(IT_DFT, [(rings(IT_DFT, 0, 2048), t["dft"][:, 0:2048]),
                           (rings(IT_DFT, 2048, 4352), t["dft"][:, 2048:4352]),
                           (wfour.rearrange("p (g d) -> p g d", g=4), t["e_w_fourier"][0].rearrange("g c d -> c g d"))])

            def load_wout(first, name, half):
                w = t[name][0].rearrange("(i p) c -> p i c", p=P)
                it = first + half
                load3(it, [(rings(it, a * D, b * D).rearrange("p (i c) -> p i c", c=D), w[:, 4 * half + a:4 * half + b, :])
                           for a, b in ((0, 2), (2, 3), (3, 4))])

            load_wout(IT_WOUT, "e_w_out", 0)
            sp.wait_ge(aT_mm, 4)
            load_wout(IT_WOUT, "e_w_out", 1)

            def load_shared(item, l):
                g, u, _ = expert(slot_of(item))
                up = t["sh_w_up"][l].rearrange("(p j) f -> p j f", j=NK)
                load3(item, [(g, t["sh_w_gate"][l].rearrange("(p j) f -> p j f", j=NK)),
                             (u[:, 0:4, :], up[:, 0:4, :]), (u[:, 4:8, :], up[:, 4:8, :])])

            load_shared(IT_SH0, 0)

            def load_expert(l, e, slot):
                g, u, d = expert(slot)
                for dst, name in ((g, "exp_w_gate"), (u, "exp_w_up")):
                    sp.dma_start(dst, t[name][l, bass.ds(e, 1), :, :].rearrange("a (p j) f -> p (a j) f", j=NK))\
                        .then_inc(slot_full[slot], 16)
                sp.dma_start(d, t["exp_w_down"][l, bass.ds(e, 1), :, :].rearrange("a (p c) d -> p (a c) d", c=FC))\
                    .then_inc(slot_full[slot], 16)

            def load_experts(l, frees):
                for u in range(SLOTS):
                    sp.wait_ge(*frees[u])
                    load_expert(l, u, slot_of(IT_EXP[l] + u))
                with sp.Fori(1, E // SLOTS) as i:
                    for u in range(SLOTS):
                        sp.wait_ge(down_mm, i * SLOTS + (l * E + u - SLOTS + 1))
                        load_expert(l, i * SLOTS + u, slot_of(IT_EXP[l] + u))

            load_experts(0, [(four_mm, 4), (wout_mm, NT), (wout_mm, NT), (shg_mm, 4)])

            def load_owin(n):
                w, col, dst = t["o_w_in"][0].rearrange("(p j) c -> p j c", j=NK), (1024, 1536, 0, 512)[n], owin(n)
                load3(IT_OWIN + n, [(dst[:, a:b, :], w[:, a:b, col:col + 512]) for a, b in ((0, 3), (3, 6), (6, 8))])

            for n in range(3):
                sp.wait_ge(down_mm, E - SLOTS + 1 + n)
                load_owin(n)
            overflow_sp(sp, 0)
            sp.sem_inc(counts_read, 1)
            sp.wait_ge(acc_in[NT - 1], 16)
            load_owin(3)
            sp.wait_ge(v_mm, NT)
            load_wout(IT_OWOUT, "o_w_out", 0)
            sp.wait_ge(v_mm, 2 * NT)
            load_wout(IT_OWOUT, "o_w_out", 1)
            sp.wait_ge(u_mm, 4)
            load_shared(IT_SH1, 1)
            load_experts(1, [(u_mm, 8), (wout_mm, 2 * NT), (wout_mm, 2 * NT), (shg_mm, 8)])
            overflow_sp(sp, 1)
            for tt in range(NT):
                sp.wait_ge(ln_done, 4 * NT + tt + 1)
                sp.dma_start(out[0, tt * P:(tt + 1) * P, :], xres[:, tt, :]).then_inc(out_done, 16)
            sp.wait_ge(out_done, 16 * NT)

        def mm(o, lhsT, rhs, first, last):
            return nc.tensor.matmul(o, lhsT, rhs, start=first, stop=last)

        @block.tensor
        def _(pe):
            def arrived(item):
                pe.wait_ge(slot_full[slot_of(item)], full_value(item))

            def transpose_x(r, tt):
                pe.wait_ge(perm_done, r * NT + tt + 1)
                for hf in range(2):
                    if tt >= 2:
                        pe.wait_ge(xT_act if hf else xT_dve, r * NT + tt - 1)
                    for k in range(4):
                        j = 4 * hf + k
                        ins = nc.tensor.transpose(ps[:, 4 + (2 * tt + hf) % 4, k * P:(k + 1) * P],
                                                  xperm[:, tt, j * P:(j + 1) * P], ident)
                    ins.then_inc(tr_done, 1)

            def xT_ready(r, tt=NT - 1):
                pe.wait_ge(xT_dve, r * NT + tt + 1)
                pe.wait_ge(xT_act, r * NT + tt + 1)

            def out_projection(r, first, ready):
                src = catT if r == 0 else uT
                for tt in range(NT):
                    if tt >= 2:
                        pe.wait_ge(resid_done, r * NT + tt - 1)
                    for hf in range(2):
                        for i in range(8):
                            if tt == 0 and hf == 0:
                                ready(i)
                            ins = mm(ps[:, 2 * (tt % 2) + hf, :], src[:, i, tt * P:(tt + 1) * P],
                                     wout(first, i)[:, hf * 512:(hf + 1) * 512], i == 0, i == 7)
                    ins.then_inc(wout_mm, 1)
                    if tt >= 1:
                        transpose_x(2 * r + 1, tt - 1)

            def moe(l):
                r = 2 * l + 1

                def logits(tt):
                    xT_ready(r, tt)
                    for j in range(NK):
                        ins = mm(ps[:, 0, tt * E:(tt + 1) * E], xT[:, j, tt * P:(tt + 1) * P], router[:, j, :],
                                 j == 0, j == NK - 1)
                    return ins

                g, u, _ = expert(slot_of(IT_SH0 if l == 0 else IT_SH1))

                def shared_in(w, c, bank, lo=0, hi=T):
                    for j in range(NK):
                        ins = mm(ps[:, bank, lo:hi], w[:, j, c::FC], xT[:, j, lo:hi], j == 0, j == NK - 1)
                    return ins

                pe.wait_ge(router_in, 32 * (l + 1))
                pe.wait_ge(resid_done, l * NT + 3)
                for tt in range(NT - 1):
                    logits(tt)
                arrived(IT_SH0 if l == 0 else IT_SH1)
                shared_in(g, 0, 1, 0, 3 * P)
                transpose_x(r, NT - 1)
                logits(NT - 1).then_inc(lg_mm, 1)
                shared_in(g, 0, 1, 3 * P, T).then_inc(shg_mm, 1)
                pe.wait_ge(resid_done, (l + 1) * NT)
                shared_in(g, 1, 2).then_inc(shg_mm, 1)
                pe.wait_ge(bconst_in, 16)
                pe.wait_ge(mask_done, l + 1)
                for tt in range(NT):
                    for t2 in range(tt + 1):
                        mm(ps[:, 5, tt * E:(tt + 1) * E], before if t2 == tt else ones, maskb[:, t2, :],
                           t2 == 0, t2 == tt)
                for tt in range(NT):
                    ins = mm(ps[:, 5, NT * E:(NT + 1) * E], ones, maskb[:, tt, :], tt == 0, tt == NT - 1)
                ins.then_inc(rk_mm, 1)
                shared_in(u, 0, 4).then_inc(shg_mm, 1)

                def slot_table(q):
                    if not (isinstance(q, int) and q == 0):
                        pe.wait_ge(idx_done, q + l * E // 4)
                    for b in range(4):
                        pe.wait_ge(pick_done, q * 4 + (l * E + b + 1))
                        for tt in range(NT):
                            ins = mm(ps[0:NB, 7, 6 * b:6 * b + 6], pick[:, b, tt, :],
                                     tab[:, tt, bass.ds(q * 4 + b, 1), :].rearrange("p a c -> p (a c)"),
                                     tt == 0, tt == NT - 1)
                        ins.then_inc(pick_mm, 1)

                pe.wait_ge(tab_done, l + 1)
                slot_table(0)
                shared_in(u, 1, 6).then_inc(shg_mm, 1)
                base = l * E

                def gathered_in(n, u):
                    pe.wait_ge(gathered[u], (n - u) * 4 + 16 * (l * E // 4 + 1))
                    if not (isinstance(n, int) and n + base == 0):
                        pe.wait_ge(xgT_dve, n + base)
                        pe.wait_ge(xgT_act, n + base)
                    for j in range(NK):
                        ins = nc.tensor.transpose(ps[:, j // 4, (j % 4) * NB:(j % 4 + 1) * NB],
                                                  xg[0:NB, u, j * P:(j + 1) * P], ident[0:NB, 0:NB])
                    ins.then_inc(xg_tr, 1)

                def shared_down(n):
                    pe.wait_ge(sh_down_in, 16 * (l + 1))
                    pe.wait_ge(sh_mul, 2 * (l + 1))
                    if n:
                        pe.wait_ge(sh_y, l * 2 * NT + n)
                    for c in range(FC):
                        ins = mm(ps[:, 6, :], sh_h[:, c, (n // 2) * P:(n // 2 + 1) * P],
                                 sh_down[:, c, (n % 2) * 512:(n % 2 + 1) * 512], c == 0, c == FC - 1)
                    ins.then_inc(shd_mm, 1)

                def expert_step(n, u, next_too, first, shared):
                    slot = slot_of(IT_EXP[l] + u)
                    b = u % 2
                    g, up, d = expert(slot)
                    pe.wait_ge(slot_full[slot], (n - u) * (PER_ITEM // SLOTS) + full_value(IT_EXP[l] + u))
                    pe.wait_ge(xgT_dve, n + (base + 1))
                    pe.wait_ge(xgT_act, n + (base + 1))
                    if not first:
                        pe.wait_ge(h_done, n + base)
                    for w, bank, s in ((g, 2, gate_mm), (up, 3, up_mm)):
                        for c in range(FC):
                            for j in range(NK):
                                ins = mm(ps[:, bank, c * NB:(c + 1) * NB], w[:, j, c::FC],
                                         xgT[:, b, j, :], j == 0, j == NK - 1)
                        ins.then_inc(s, 1)
                    if next_too:
                        gathered_in(n + 1, (u + 1) % SLOTS)
                    if shared:
                        shared_down(n)
                    pe.wait_ge(h_done, n + (base + 1))
                    if not first:
                        pe.wait_ge(y_dve, n + base)
                        pe.wait_ge(y_act, n + base)
                    for hf in range(2):
                        for c in range(FC):
                            ins = mm(ps[0:NB, 4 + hf, :], hT[:, b, c, :], d[:, c, hf * 512:(hf + 1) * 512],
                                     c == 0, c == FC - 1)
                    ins.then_inc(down_mm, 1)

                pe.wait_ge(sh_silu, 2 * (l + 1))
                gathered_in(0, 0)
                pe.wait_ge(counts_ready, l + 1)
                pe.wait_ge(sh_mul, 2 * (l + 1))
                for q in range(2):
                    slot_table(q + 1)
                    for u in range(SLOTS):
                        expert_step(q * SLOTS + u, u, True, q + u == 0, True)
                with pe.Fori(2, QUADS - 1) as q:
                    slot_table(q + 1)
                    for u in range(SLOTS):
                        expert_step(q * SLOTS + u, u, True, False, False)
                for u in range(SLOTS):
                    expert_step(E - SLOTS + u, u, u < SLOTS - 1, False, False)
                overflow_pe(pe, l)

            pe.wait_ge(const_in, 16)
            def qkv_part(tt, js):
                b0 = 2 * (tt % 2)
                for bank, lo, hi in ((0, 512, 1024), (1, 1024, 1280)):
                    for j in js:
                        ins = mm(ps[:, b0 + bank, 0:hi - lo], xT[:, j, tt * P:(tt + 1) * P],
                                 win(j)[:, lo:hi], j == 0, j == NK - 1)
                return ins

            transpose_x(0, 0)
            transpose_x(0, 1)
            arrived(IT_WIN)
            xT_ready(0, 0)
            qkv_part(0, range(4))
            transpose_x(0, 2)
            xT_ready(0, 1)
            qkv_part(1, range(4))
            transpose_x(0, 3)
            arrived(IT_WIN + 1)
            for tt in range(2):
                qkv_part(tt, range(4, NK)).then_inc(qkv_mm, 1)
            for tt in range(2, NT):
                xT_ready(0, tt)
                pe.wait_ge(qkv_cp, tt - 1)
                qkv_part(tt, range(NK)).then_inc(qkv_mm, 1)
            for g in range(4):
                for j in range(NK):
                    ins = mm(ps[:, 4 + g, :], win(j)[:, g * P:(g + 1) * P], xT[:, j, :], j == 0, j == NK - 1)
                ins.then_inc(aT_mm, 1)
            arrived(IT_DFT)
            pe.wait_ge(aT_cp, 2)
            mm(ps[:, 4, :], chn_c, wfour, True, True)
            mm(ps[:, 5, :], chn_s, wfour, True, True).then_inc(fw_mm, 1)
            pe.wait_ge(aT_cp, 4)
            pe.wait_ge(fw_cp, 2)
            for tt in range(NT):
                if tt >= 2:
                    pe.wait_ge(z_cp, tt - 1)
                for g in range(4):
                    ins = mm(ps[:, 6 - 2 * (tt % 2) + g // 2, (g % 2) * 256:(g % 2 + 1) * 256],
                             aT[:, g, tt * P:(tt + 1) * P], fw[:, g, :, :].rearrange("p s d -> p (s d)"), True, True)
                ins.then_inc(z_mm, 1)
            pe.wait_ge(z_cp, NT)
            pe.wait_ge(qkv_cp, NT)

            def positions(g, lo=0, hi=NT):
                bank = (0, 1, 2, 7)[g]
                for tt in range(lo, hi):
                    mm(ps[:, bank, :], zmix[:, tt, g, 0, :], dft_c[:, tt, :], tt == 0, False)
                    ins = mm(ps[:, bank, :], zmix[:, tt, g, 1, :], dft_s[:, tt, :], False, tt == NT - 1)
                if hi == NT:
                    ins.then_inc(four_mm, 1)

            def turn_qk(tt):
                pe.wait_ge(rot_done, tt + 1)
                if tt >= 2:
                    pe.wait_ge(qkT_cp, tt - 1)
                for i in range(5):
                    n = 8 * (tt % 2) + i
                    ins = nc.tensor.transpose(ps[:, 4 + n // 4, (n % 4) * P:(n % 4 + 1) * P],
                                              rot[:, tt, i * P:(i + 1) * P], ident)
                ins.then_inc(qkT_tr, 1)

            positions(0)
            positions(1)
            turn_qk(0)
            turn_qk(1)
            positions(2)
            turn_qk(2)
            turn_qk(3)
            pe.wait_ge(qkT_cp, NT)
            pe.wait_ge(four_cp, 3)

            def score(n):
                i, k = n // 8, n % 8
                hh, tt = k // NT, k % NT
                if n >= 2:
                    pe.wait_ge(p_done, n - 1)
                mm(ps[:, n % 2, :], qkT[64 * hh:64 * hh + 64, i, tt * P:(tt + 1) * P],
                   qkT[64 * hh:64 * hh + 64, 4, :], True, True).then_inc(s_mm, 1)

            def turn(n):
                pe.wait_ge(p_done, n + 1)
                if n >= 2:
                    pe.wait_ge(pT_cp, n - 1)
                for c in range(4):
                    ins = nc.tensor.transpose(ps[:, 2 + n % 2, c * P:(c + 1) * P], probs[:, n % 2, c * P:(c + 1) * P], ident)
                ins.then_inc(pT_tr, 1)

            def values(n):
                hh = n % 8 // NT
                pe.wait_ge(pT_cp, n + 1)
                if n >= 2:
                    pe.wait_ge(o_cp, n - 1)
                for c in range(4):
                    ins = mm(ps[:, 4 + n % 2, 0:64], probsT[:, n % 2, c, :], qkv[:, c, 640 + 64 * hh:704 + 64 * hh], c == 0, c == 3)
                ins.then_inc(o_mm, 1)

            units = 8 * PAIRS
            for n in range(units + 2):
                if n < units:
                    score(n)
                if n == 1:
                    positions(3)
                if 0 <= n - 1 < units:
                    turn(n - 1)
                if n >= 2:
                    values(n - 2)
            pe.wait_ge(o_cp, units)
            pe.wait_ge(four_cp, 4)
            for tt in range(NT):
                if tt >= 2:
                    pe.wait_ge(atT_cp, tt - 1)
                for i in range(4):
                    ins = nc.tensor.transpose(ps[:, 6 + tt % 2, i * P:(i + 1) * P], attn[:, tt, i * P:(i + 1) * P], ident)
                ins.then_inc(atT_tr, 1)
            arrived(IT_WOUT)
            arrived(IT_WOUT + 1)
            pe.wait_ge(atT_cp, NT)
            out_projection(0, IT_WOUT, lambda i: None)
            moe(0)

            def v_half(n, tt):
                xT_ready(2, tt)
                if n == 1:
                    pe.wait_ge(v_pre, tt + 1)
                for j in range(NK):
                    ins = mm(ps[:, tt, :], xT[:, j, tt * P:(tt + 1) * P], owin(n)[:, j, :], j == 0, j == NK - 1)
                ins.then_inc(v_mm, 1)

            transpose_x(2, 0)
            arrived(IT_OWIN)
            for tt in range(NT):
                if tt < NT - 1:
                    transpose_x(2, tt + 1)
                v_half(0, tt)
            pe.wait_ge(small_in, 96)
            for hf in range(2):
                for g in range(4):
                    ins = nc.tensor.transpose(ps[:, 4 + hf, g * P:(g + 1) * P], ws[:, 4 * hf + g, :], ident)
                ins.then_inc(wsT_tr, 1)
            arrived(IT_OWIN + 1)
            for tt in range(NT):
                v_half(1, tt)
            pe.wait_ge(wsT_cp, 2)
            for n in range(8):
                if n % 4 == 0:
                    arrived(IT_OWIN + 2 + n // 4)
                if n >= 4:
                    pe.wait_ge(u_act, n - 3)
                for j in range(NK):
                    ins = mm(ps[:, 4 + n % 4, :], owin(2 + n // 4)[:, j, (n % 4) * P:(n % 4 + 1) * P], xT[:, j, :],
                             j == 0, j == NK - 1)
                ins.then_inc(u_mm, 1)
            pe.wait_ge(vln_done, NT)
            for g in range(CH):
                if g == 4:
                    pe.wait_ge(u_act, CH)
                for tt in range(NT):
                    ins = mm(ps[:, g, tt * P:(tt + 1) * P], vn[:, tt, g * P:(g + 1) * P], wsT[:, g, :], True, True)
                ins.then_inc(sp_mm, 1)
            arrived(IT_OWOUT)
            arrived(IT_OWOUT + 1)
            out_projection(1, IT_OWOUT, lambda i: pe.wait_ge(uv_done, i + 1))
            moe(1)

        @block.scalar
        def _(act):
            norms = [None, ("ln_mix_g", "ln_mix_b", 0), ("ln_ffn_g", "ln_ffn_b", 0),
                     ("o_v_ln_g", "o_v_ln_b", 0), ("ln_mix_g", "ln_mix_b", 1), ("ln_ffn_g", "ln_ffn_b", 1)]

            def load_norm(k):
                for a in range(2):
                    act.dma_start(lnp[:, a, :], t[norms[k][a]][norms[k][2]].partition_broadcast(P)).then_inc(lnp_in, 16)

            act.dma_start(consts[:], t["consts"]).then_inc(const_in, 16)
            for a, name in enumerate(("e_q_gain", "e_k_gain")):
                act.dma_start(gains[:, a, :], t[name][0].partition_broadcast(P)).then_inc(small_in, 16)

            def root(k, tt):
                act.wait_ge(ln_stats, k * NT + tt + 1)
                nc.scalar.activation(std[:, tt:tt + 1], vare[:, tt:tt + 1], ACT.Sqrt).then_inc(ln_std, 1)

            def permute(r, tt):
                act.wait_ge(ln_done, r * NT + tt + 1)
                nc.scalar.activation(xperm[:, tt, :].rearrange("q (j p) -> q p j", p=P),
                                     xres[:, tt, :].rearrange("q (p j) -> q p j", p=P), ACT.Copy).then_inc(perm_done, 1)

            def copy_xT(r, tt):
                act.wait_ge(tr_done, r * 2 * NT + 2 * tt + 2)
                nc.scalar.activation(xT[:, 4:8, tt * P:(tt + 1) * P],
                                     ps[:, 4 + (2 * tt + 1) % 4, :].rearrange("p (k q) -> p k q", k=4), ACT.Copy)\
                    .then_inc(xT_act, 1)

            def norm_and_turn(r):
                for s in range(NT + 1):
                    if s < NT:
                        root(r, s)
                    if s >= 1:
                        copy_xT(r, s - 1)
                    if s < NT:
                        permute(r, s)

            def moe(l):
                norm_and_turn(2 * l + 1)
                act.wait_ge(ln_done, (2 * l + 2) * NT)
                load_norm(2 if l == 0 else 5)
                act.wait_ge(lg_mm, l + 1)
                nc.scalar.activation(scores, ps[:, 0, 0:NT * E].rearrange("p (t e) -> p t e", t=NT), ACT.Sigmoid)\
                    .then_inc(sg_done, 1)
                for c in range(FC):
                    act.wait_ge(shg_mm, 4 * l + c + 1)
                    nc.scalar.activation(sh_sil[:, c, :], ps[:, 1 + c, :], ACT.Silu).then_inc(sh_silu, 1)
                act.wait_ge(shg_mm, 4 * (l + 1))
                act.dma_start(sh_down, t["sh_w_down"][l].rearrange("(p c) d -> p c d", c=FC)).then_inc(sh_down_in, 16)
                base = l * E

                def copy_tokens(n, b, first):
                    act.wait_ge(xg_tr, n + (base + 1))
                    if not first:
                        act.wait_ge(up_mm, n + (base - 1))
                    nc.scalar.activation(xgT[:, b, 4:8, :], ps[:, 1, 0:4 * NB].rearrange("p (k s) -> p k s", k=4),
                                         ACT.Copy).then_inc(xgT_act, 1)

                def expert_step(n, u, next_too, first):
                    b = u % 2
                    act.wait_ge(gate_mm, n + (base + 1))
                    if not (first and u < 2):
                        act.wait_ge(h_done, n + (base - 1))
                    nc.scalar.activation(sil[:, b, :, :], ps[:, 2, 0:FC * NB].rearrange("p (c s) -> p c s", c=FC), ACT.Silu)\
                        .then_inc(silu_done, 1)
                    if next_too:
                        copy_tokens(n + 1, 1 - b, first and u == 0)
                    act.wait_ge(down_mm, n + (base + 1))
                    if not (first and u < 2):
                        act.wait_ge(scattered[b], (n - b) * 8 + 16 * (l * E // 2))
                    nc.scalar.activation(ysb[0:NB, b, 512:1024], ps[0:NB, 5, :], ACT.Copy,
                                         scale=w_slot[0:NB, bass.ds(n, 1)]).then_inc(y_act, 1)

                def quad(q, first, last):
                    act.wait_ge(idx_done, q + (l * QUADS + 1))
                    for u in range(SLOTS):
                        expert_step(q * SLOTS + u, u, not last or u < SLOTS - 1, first)

                copy_tokens(0, 0, True)
                quad(0, True, False)
                with act.Fori(1, QUADS - 1) as q:
                    quad(q, False, False)
                quad(QUADS - 1, False, True)
                overflow_act(act, l)
                act.wait_ge(acc_ready, l + 1)
                for tt in range(NT):
                    act.dma_start(xperm[:, tt, :], acc[l][tt * P:(tt + 1) * P, :]).then_inc(acc_in[tt], 16)

            norm_and_turn(0)
            act.wait_ge(ln_done, NT)
            load_norm(1)
            for g in range(4):
                act.wait_ge(aT_mm, g + 1)
                nc.scalar.activation(aT[:, g, :], ps[:, 4 + g, :], ACT.Copy).then_inc(aT_cp, 1)
            for a in range(2):
                act.wait_ge(fw_mm, 1)
                nc.scalar.activation(fw[:, :, a, :], ps[:, 4 + a, :].rearrange("p (g d) -> p g d", g=4), ACT.Copy)\
                    .then_inc(fw_cp, 1)
            for tt in range(NT):
                act.wait_ge(z_mm, tt + 1)
                nc.scalar.activation(zmix[:, tt, :, :, :].rearrange("p g s d -> p (g s d)"),
                                     ps[:, 6 - 2 * (tt % 2):8 - 2 * (tt % 2), :].rearrange("p b c -> p (b c)"), ACT.Copy)\
                    .then_inc(z_cp, 1)
            act.wait_ge(qk_ssq, 1)
            nc.scalar.activation(qk_rs, qk_ss, ACT.Sqrt).then_inc(qk_root, 1)

            def copy_positions(g):
                act.wait_ge(four_mm, g + 1)
                nc.scalar.activation(catT[:, g, :], ps[:, (0, 1, 2, 7)[g], :], ACT.Copy).then_inc(four_cp, 1)

            for g in range(3):
                copy_positions(g)

            act.wait_ge(rot_done, NT)

            def load_router(l):
                act.dma_start(router, t["router_w"][l].rearrange("(p j) e -> p j e", j=NK)).then_inc(router_in, 16)
                act.dma_start(rb_w, t["router_b"][l].partition_broadcast(P)).then_inc(router_in, 16)

            load_router(0)

            def exps(n, k, first):
                act.wait_ge(max_done, n + 1)
                if not (first and k < 2):
                    act.wait_ge(pT_tr, n - 1)
                if not (first and k < 4):
                    act.wait_ge(o_cp, n - 3)
                nc.scalar.activation(probs[:, k % 2, :], ps[:, k % 2, :], ACT.Exp, bias=nmax[:, k % 2:k % 2 + 1],
                                     accum_out=rsum[:, k % 4:k % 4 + 1]).then_inc(p_done, 1)

            def copy_pT(n, k, first):
                act.wait_ge(pT_tr, n + 1)
                if not (first and k < 2):
                    act.wait_ge(o_mm, n - 1)
                nc.scalar.activation(probsT[:, k % 2, :, :].rearrange("p c q -> p (c q)"), ps[:, 2 + k % 2, :], ACT.Copy)\
                    .then_inc(pT_cp, 1)

            act.wait_ge(z_cp, NT)
            for k in range(8):
                exps(k, k, True)
                if k == 1:
                    copy_positions(3)
                if k >= 1:
                    copy_pT(k - 1, k - 1, True)
            with act.Fori(1, PAIRS) as i:
                for k in range(8):
                    exps(i * 8 + k, k, False)
                    copy_pT(i * 8 + (k - 1), (k - 1) % 8, False)
            copy_pT(8 * PAIRS - 1, 7, False)
            moe(0)

            act.dma_start(ws, t["o_w_spatial"][0].rearrange("g p q -> p g q")).then_inc(small_in, 16)
            act.dma_start(bv_w, t["o_b_in"][0, D:2 * D].partition_broadcast(P)).then_inc(small_in, 16)
            act.dma_start(bs_w, t["o_b_spatial"][0].rearrange("g q -> (g q)").partition_broadcast(P)).then_inc(small_in, 16)
            act.dma_start(bu_col, t["u_bias"]).then_inc(small_in, 16)
            load_router(1)
            norm_and_turn(2)
            act.wait_ge(ln_done, 3 * NT)
            load_norm(3)

            def v_gelu(n):
                act.wait_ge(v_pre, n + 1)
                half = vn[:, n % NT, (n // NT) * 512:(n // NT + 1) * 512]
                nc.scalar.activation(half, half, ACT.Gelu).then_inc(v_act, 1)

            for tt in range(NT):
                v_gelu(tt)
            for hf in range(2):
                act.wait_ge(wsT_tr, hf + 1)
                nc.scalar.activation(wsT[:, 4 * hf:4 * hf + 4, :], ps[:, 4 + hf, :].rearrange("p (g q) -> p g q", g=4),
                                     ACT.Copy).then_inc(wsT_cp, 1)
            for tt in range(NT + 1):
                if tt < NT:
                    v_gelu(NT + tt)
                if tt >= 1:
                    act.wait_ge(vln_stats, tt)
                    nc.scalar.activation(std[:, tt - 1:tt], vare[:, tt - 1:tt], ACT.Sqrt).then_inc(vln_std, 1)
            act.wait_ge(small_in, 96)
            for n in range(8):
                act.wait_ge(u_mm, n + 1)
                nc.scalar.activation(uT[:, n, :], ps[:, 4 + n % 4, :], ACT.Gelu, bias=bu_col[:, n:n + 1]).then_inc(u_act, 1)
            act.wait_ge(vln_done, NT)
            load_norm(4)
            moe(1)
            for tt in range(NT):
                root(4, tt)

        @block.vector
        def _(dve):
            step = Steps(dve, dve_step)

            def norm_stats(src, tt, stats_sem):
                if step.n:
                    step.wait()
                for hf in range(2):
                    step.done(nc.vector.bn_stats(stats[:, tt, hf, :], src[:, tt, hf * 512:(hf + 1) * 512]))
                step.wait()
                step.done(nc.vector.bn_aggr(mv[:, tt, :], stats[:, tt, :, :].rearrange("p h s -> p (h s)")))
                step.wait()
                nc.vector.tensor_scalar(vare[:, tt:tt + 1], mv[:, tt, 1:2], LN_EPS, None, ALU.add).then_inc(stats_sem, 1)

            def norm_apply(src, tt, std_sem, std_value, order, done_sem):
                dve.wait_ge(std_sem, std_value)
                step.done(nc.vector.reciprocal(rstd[:, tt:tt + 1], std[:, tt:tt + 1]))
                dve.wait_ge(lnp_in, 32 * (order + 1))
                step.done(nc.vector.scalar_tensor_tensor(src[:, tt, :], src[:, tt, :], mv[:, tt, 0:1], lnp[:, 0, :],
                                                         ALU.subtract, ALU.mult))
                step.wait()
                nc.vector.scalar_tensor_tensor(src[:, tt, :], src[:, tt, :], rstd[:, tt:tt + 1], lnp[:, 1, :],
                                               ALU.mult, ALU.add).then_inc(done_sem, 1)

            def copy_xT(r, tt):
                dve.wait_ge(tr_done, r * 2 * NT + 2 * tt + 1)
                nc.vector.tensor_copy(xT[:, 0:4, tt * P:(tt + 1) * P],
                                      ps[:, 4 + 2 * tt % 4, :].rearrange("p (k q) -> p k q", k=4)).then_inc(xT_dve, 1)

            def norm(r, order, before_tile):
                for s in range(NT + 1):
                    if s < NT:
                        before_tile(s)
                        norm_stats(xres, s, ln_stats)
                    if s >= 1:
                        copy_xT(r, s - 1)
                    if s < NT:
                        norm_apply(xres, s, ln_std, r * NT + s + 1, order, ln_done)
                dve.wait_ge(ln_done, (r + 1) * NT)

            def add_projection(r):
                def tile(tt):
                    dve.wait_ge(wout_mm, r * NT + tt + 1)
                    nc.vector.scalar_tensor_tensor(xres[:, tt, :], xres[:, tt, :], ALPHA,
                                                   ps[:, 2 * (tt % 2):2 * (tt % 2) + 2, :].rearrange("p b c -> p (b c)"),
                                                   ALU.mult, ALU.add).then_inc(resid_done, 1)
                    dve.wait_ge(resid_done, r * NT + tt + 1)
                return tile

            def sum_ready(l):
                def tile(tt):
                    if tt == 0:
                        dve.wait_ge(acc_in[0], 16 * (l + 1))
                        nc.vector.tensor_tensor(xres[:, 0, :], xres[:, 0, :], xperm[:, 0, :], ALU.add).then_inc(first_sum, 1)
                        dve.wait_ge(first_sum, l + 1)
                    else:
                        dve.wait_ge(acc_sum, l * (NT - 1) + tt)
                return tile

            def bc(ap, shape):
                return ap.to_broadcast(shape)

            def moe(l):
                norm(1 + 2 * l, 1 if l == 0 else 4, add_projection(l))
                dve.wait_ge(bconst_in, 16)
                step.done(nc.vector.tensor_copy(tab[:, :, :, 0:3].rearrange("p t e c -> p t e c"),
                                                bc(posb.unsqueeze(2), [P, NT, E, 3])))
                dve.wait_ge(sg_done, l + 1)
                dve.wait_ge(router_in, 32 * (l + 1))
                step.done(nc.vector.tensor_tensor(sel, scores, bc(rb_w.unsqueeze(1), [P, NT, E]), ALU.add))
                step.wait()
                for tt in range(NT):
                    for g in range(N_EGROUPS):
                        step.done(nc.vector.max(m8[:, tt, g, :], sel[:, tt, g * 8:(g + 1) * 8]))
                step.wait()
                step.done(nc.vector.tensor_tensor(gsc, m8[:, :, :, 0], m8[:, :, :, 1], ALU.add))
                step.wait()
                mine, other = bc(gsc.unsqueeze(3), [P, NT, 8, 8]), bc(gsc.unsqueeze(2), [P, NT, 8, 8])
                step.done(nc.vector.tensor_tensor(cmps[0], other, mine, ALU.is_gt))
                step.done(nc.vector.tensor_tensor(cmps[1], other, mine, ALU.is_equal))
                step.wait()
                step.done(nc.vector.tensor_tensor(cmps[2], cmps[1], bc(earlier.unsqueeze(1), [P, NT, 8, 8]), ALU.mult))
                step.wait()
                step.done(nc.vector.tensor_tensor(cmps[1], cmps[0], cmps[2], ALU.add))
                step.wait()
                step.done(nc.vector.tensor_reduce(grank, cmps[1], AX, ALU.add))
                step.wait()
                step.done(nc.vector.tensor_scalar(gmask, grank, float(TOPK_GROUPS), None, ALU.is_lt))
                step.wait()
                step.done(nc.vector.tensor_scalar(gpen, gmask, BIG, BIG, ALU.mult, ALU.subtract))
                by_group = "p t (g k) -> p t g k"
                step.done(nc.vector.tensor_tensor(selm.rearrange(by_group, g=8), sel.rearrange(by_group, g=8),
                                                  bc(gmask.unsqueeze(3), [P, NT, 8, 8]), ALU.mult))
                step.wait()
                step.done(nc.vector.tensor_tensor(sel.rearrange(by_group, g=8), selm.rearrange(by_group, g=8),
                                                  bc(gpen.unsqueeze(3), [P, NT, 8, 8]), ALU.add))
                step.wait()
                for tt in range(NT):
                    step.done(nc.vector.max(v8[:, tt, :], sel[:, tt, :]))
                step.wait()
                for tt in range(NT):
                    step.done(nc.vector.match_replace(rep[:, tt, :], v8[:, tt, :], sel[:, tt, :], -3.0 * BIG))
                step.wait()
                nc.vector.tensor_scalar(maskb, rep, -2.0 * BIG, None, ALU.is_lt).then_inc(mask_done, 1)
                step.done(nc.vector.tensor_scalar(selm, rep, -2.0 * BIG, None, ALU.is_lt))
                step.wait()
                step.done(nc.vector.tensor_tensor(rep, scores, selm, ALU.mult))
                step.wait()
                step.done(nc.vector.tensor_reduce(wsum, rep, AX, ALU.add))
                step.wait()
                step.done(nc.vector.reciprocal(wfac, wsum))
                step.wait()
                step.done(nc.vector.tensor_scalar(wsum, wfac, ROUTE_SCALE, None, ALU.mult))
                step.wait()
                step.done(nc.vector.tensor_tensor(sel, rep, bc(wsum.unsqueeze(2), [P, NT, E]), ALU.mult))
                step.wait()
                step.done(nc.vector.tensor_copy(tab[:, :, :, 3], sel))
                step.wait()
                step.done(nc.vector.tensor_tensor(rep, sel, tab[:, :, :, 3], ALU.subtract))
                step.wait()
                step.done(nc.vector.tensor_copy(tab[:, :, :, 4], rep))
                step.wait()
                step.done(nc.vector.tensor_tensor(sel, rep, tab[:, :, :, 4], ALU.subtract))
                step.wait()
                nc.vector.tensor_copy(tab[:, :, :, 5], sel).then_inc(tab_done, 1)
                dve.wait_ge(rk_mm, l + 1)
                step.done(nc.vector.scalar_tensor_tensor(rep, ps[:, 5, 0:NT * E].rearrange("p (t e) -> p t e", t=NT), 1.0,
                                                         selm, ALU.add, ALU.mult))
                step.done(nc.vector.tensor_copy(cnt_tab, ps[:, 5, NT * E:(NT + 1) * E]))
                step.done(nc.vector.tensor_reduce(idx_f[:, 0:1], ps[:, 5, NT * E:(NT + 1) * E], AX, ALU.max))
                step.wait()
                nc.vector.tensor_copy(cnt_max, idx_f[:, 0:1]).then_inc(counts_ready, 1)
                step.done(nc.vector.tensor_scalar(rankm, rep, -1.0, None, ALU.add))
                step.wait()

                def choose(e, b, first):
                    if not first:
                        dve.wait_ge(pick_mm, e + (l * E - 3))
                    nc.vector.tensor_tensor(pick[:, b, :, :], bc(rankm[:, :, bass.ds(e, 1)], [P, NT, NB]),
                                            bc(iota.unsqueeze(1), [P, NT, NB]), ALU.is_equal).then_inc(pick_done, 1)

                def slot_table(q, first):
                    base = l * QUADS
                    dve.wait_ge(pick_mm, q * 4 + (l * E + 4))
                    if not first:
                        dve.wait_ge(idx_done, q + base)
                    nc.vector.tensor_copy(pi_w[0:NB, 0:24], ps[0:NB, 7, 0:24]).then_inc(pi_cp, 1)
                    dve.wait_ge(pi_cp, q + (base + 1))
                    v = pi[0:NB, :, :]
                    nc.vector.scalar_tensor_tensor(pi_idx[0:NB, :], v[:, :, 2], negslot[0:NB, :], v[:, :, 0],
                                                   ALU.mult, ALU.add)
                    nc.vector.tensor_tensor(pi_wt[0:NB, :], v[:, :, 3], v[:, :, 4], ALU.add).then_inc(pi_mid, 1)
                    dve.wait_ge(pi_mid, q + (base + 1))
                    nc.vector.scalar_tensor_tensor(idx_tab[0:NB, bass.ds(q * 4, 4)], pi_idx[0:NB, :], dump[0:NB, :],
                                                   v[:, :, 1], ALU.add, ALU.add)
                    nc.vector.tensor_tensor(w_slot[0:NB, bass.ds(q * 4, 4)], pi_wt[0:NB, :], v[:, :, 5], ALU.add)\
                        .then_inc(idx_done, 1)

                def shared_mul(c):
                    dve.wait_ge(sh_silu, 2 * l + c + 1)
                    dve.wait_ge(shg_mm, 4 * l + 3 + c)
                    nc.vector.tensor_tensor(sh_h[:, c, :], sh_sil[:, c, :], ps[:, 4 + 2 * c, :], ALU.mult).then_inc(sh_mul, 1)

                for b in range(4):
                    choose(b, b, True)
                slot_table(0, True)
                shared_mul(0)
                for b in range(4):
                    choose(4 + b, b, False)
                shared_mul(1)

                def add_shared(n):
                    dve.wait_ge(shd_mm, l * 2 * NT + n + 1)
                    half = xres[:, n // 2, (n % 2) * 512:(n % 2 + 1) * 512]
                    nc.vector.scalar_tensor_tensor(half, half, ALPHA, ps[:, 6, :], ALU.mult, ALU.add).then_inc(sh_y, 1)

                base = l * E

                def copy_tokens(n, b, first):
                    dve.wait_ge(xg_tr, n + (base + 1))
                    if not first:
                        dve.wait_ge(up_mm, n + (base - 1))
                    nc.vector.tensor_copy(xgT[:, b, 0:4, :], ps[:, 0, 0:4 * NB].rearrange("p (k s) -> p k s", k=4))\
                        .then_inc(xgT_dve, 1)

                def expert_step(n, u, next_too, first, between):
                    b = u % 2
                    dve.wait_ge(silu_done, n + (base + 1))
                    dve.wait_ge(up_mm, n + (base + 1))
                    if not (first and u < 2):
                        dve.wait_ge(down_mm, n + (base - 1))
                    nc.vector.tensor_tensor(hT[:, b, :, :], sil[:, b, :, :],
                                            ps[:, 3, 0:FC * NB].rearrange("p (c s) -> p c s", c=FC), ALU.mult)\
                        .then_inc(h_done, 1)
                    if next_too:
                        copy_tokens(n + 1, 1 - b, first and u == 0)
                    between()
                    dve.wait_ge(down_mm, n + (base + 1))
                    if not (first and u < 2):
                        dve.wait_ge(scattered[b], (n - b) * 8 + 16 * (l * E // 2))
                    nc.vector.tensor_scalar(ysb[0:NB, b, 0:512], ps[0:NB, 4, :], w_slot[0:NB, bass.ds(n, 1)], None, ALU.mult)\
                        .then_inc(y_dve, 1)

                def quad(q, first=False, shared=False, last=0):
                    for u in range(SLOTS):
                        def between():
                            if u == 0 and last < 2:
                                slot_table(q + 1, False)
                            if last < 1:
                                choose(q * 4 + (8 + u), u, False)
                            if shared:
                                add_shared(q * 4 + u)
                        expert_step(q * SLOTS + u, u, last < 2 or u < SLOTS - 1, first, between)

                copy_tokens(0, 0, True)
                quad(0, first=True, shared=True)
                quad(1, shared=True)
                with dve.Fori(2, QUADS - 2) as q:
                    quad(q)
                quad(QUADS - 2, last=1)
                quad(QUADS - 1, last=2)
                overflow_dve(dve, step, l)
                dve.wait_ge(sh_y, 2 * NT * (l + 1))

            norm(0, 0, lambda tt: dve.wait_ge(x_in[tt], 16))
            dve.wait_ge(const_in, 16)
            dve.wait_ge(small_in, 32)
            step.done(nc.vector.tensor_scalar(gains[:, 0, :], gains[:, 0, :], HEAD_DIM ** -0.5, None, ALU.mult))
            for tt in range(NT):
                dve.wait_ge(qkv_mm, tt + 1)
                b0 = 2 * (tt % 2)
                nc.vector.tensor_copy(qkv[:, tt, :], ps[:, b0:b0 + 2, :].rearrange("p b c -> p (b c)")[:, 0:QKV_WIDTH])\
                    .then_inc(qkv_cp, 1)
            for tt in range(NT):
                dve.wait_ge(qkv_cp, tt + 1)
                step.wait()
                step.done(nc.vector.tensor_tensor(tmp1, qkv[:, tt, 0:640], qkv[:, tt, 0:640], ALU.mult))
                step.wait()
                step.done(nc.vector.tensor_reduce(qk_rs[:, tt * 10:(tt + 1) * 10], tmp1.rearrange("p (h d) -> p h d", h=10),
                                                  AX, ALU.add))
            step.wait()
            nc.vector.tensor_scalar(qk_ss, qk_rs, 1.0 / HEAD_DIM, QK_EPS, ALU.mult, ALU.add).then_inc(qk_ssq, 1)
            dve.wait_ge(qk_root, 1)
            step.done(nc.vector.reciprocal(qk_ss, qk_rs))
            step.wait()
            for tt in range(NT):
                x = qkv[:, tt, 0:640]
                xh = x.rearrange("p (h d) -> p h d", h=10)
                step.done(nc.vector.tensor_tensor(tmp1.rearrange("p (h d) -> p h d", h=10), xh,
                                                  bc(qk_ss[:, tt * 10:(tt + 1) * 10].unsqueeze(2), [P, 10, 64]), ALU.mult))
                step.wait()
                for a, lo, hi in ((0, 0, 8), (1, 8, 10)):
                    step.done(nc.vector.tensor_tensor(xh[:, lo:hi, :], tmp1.rearrange("p (h d) -> p h d", h=10)[:, lo:hi, :],
                                                      bc(gains[:, a:a + 1, :], [P, hi - lo, 64]), ALU.mult))
                step.wait()
                step.done(nc.vector.tensor_tensor(tmp1.rearrange("p (h d) -> p h d", h=10), xh,
                                                  bc(rope_c[:, tt:tt + 1, :], [P, 10, 64]), ALU.mult))
                sv = rope_s[:, tt, :].rearrange("p (a r k) -> p a r k", a=2, r=2)
                for r in range(2):
                    for a in range(2):
                        step.done(nc.vector.tensor_tensor(
                            tmp2.rearrange("p (h a r k) -> p h a r k", h=10, a=2, r=2)[:, :, a, r, :],
                            x.rearrange("p (h a r k) -> p h a r k", h=10, a=2, r=2)[:, :, a, 1 - r, :],
                            bc(sv[:, a, r, :].unsqueeze(1), [P, 10, 16]), ALU.mult))
                step.wait()
                pair = "p (w i d) -> p w i d"
                step.done(nc.vector.tensor_tensor(rot[:, tt, 0:512].rearrange("p (i w d) -> p w i d", i=4, w=2),
                                                  tmp1[:, 0:512].rearrange(pair, w=2, i=4),
                                                  tmp2[:, 0:512].rearrange(pair, w=2, i=4), ALU.add))
                nc.vector.tensor_tensor(rot[:, tt, 512:640], tmp1[:, 512:640], tmp2[:, 512:640], ALU.add).then_inc(rot_done, 1)
                dve.wait_ge(rot_done, tt + 1)
                step.wait()
            for tt in range(NT):
                dve.wait_ge(qkT_tr, tt + 1)
                b0 = 4 + 2 * (tt % 2)
                nc.vector.tensor_copy(qkT[:, :, tt * P:(tt + 1) * P],
                                      ps[:, b0:b0 + 2, :].rearrange("p b c -> p (b c)")[:, 0:640]
                                      .rearrange("p (i q) -> p i q", i=5)).then_inc(qkT_cp, 1)

            def row_max(n, k, first):
                dve.wait_ge(s_mm, n + 1)
                if not (first and k < 2):
                    dve.wait_ge(p_done, n - 1)
                nc.vector.tensor_reduce(nmax[:, k % 2:k % 2 + 1], ps[:, k % 2, :], AX, ALU.max, negate=True).then_inc(max_done, 1)

            def head_out(i, n, k, first):
                dve.wait_ge(p_done, n + 1)
                dve.wait_ge(o_mm, n + 1)
                hh, tt = k // NT, k % NT
                if not (first and k < 2):
                    dve.wait_ge(o_cp, n - 1)
                nc.vector.reciprocal(rinv[:, k % 2:k % 2 + 1], rsum[:, k % 4:k % 4 + 1]).then_inc(rinv_done, 1)
                dve.wait_ge(rinv_done, n + 1)
                nc.vector.tensor_scalar(attn[:, tt, bass.ds(i * 64 + 256 * hh, 64)], ps[:, 4 + k % 2, 0:64],
                                        rinv[:, k % 2:k % 2 + 1], None, ALU.mult).then_inc(o_cp, 1)

            for k in range(8):
                row_max(k, k, True)
                if k >= 2:
                    head_out(0, k - 2, k - 2, True)
            with dve.Fori(1, PAIRS) as i:
                for k in range(8):
                    row_max(i * 8 + k, k, False)
                    if k < 2:
                        head_out(i - 1, i * 8 + (k - 2), k + 6, False)
                    else:
                        head_out(i, i * 8 + (k - 2), k - 2, False)
            for k in (6, 7):
                head_out(PAIRS - 1, 8 * (PAIRS - 1) + k, k, False)
            for tt in range(NT):
                dve.wait_ge(atT_tr, tt + 1)
                nc.vector.tensor_copy(catT[:, 4:8, tt * P:(tt + 1) * P],
                                      ps[:, 6 + tt % 2, :].rearrange("p (i q) -> p i q", i=4)).then_inc(atT_cp, 1)
            moe(0)

            norm(2, 2, sum_ready(0))
            dve.wait_ge(small_in, 96)

            dve.wait_ge(counts_read, 1)

            def v_bias(n):
                dve.wait_ge(v_mm, n + 1)
                cols = slice((n // NT) * 512, (n // NT + 1) * 512)
                nc.vector.tensor_tensor(vn[:, n % NT, cols], ps[:, n % NT, :], bv_w[:, cols], ALU.add).then_inc(v_pre, 1)

            for tt in range(NT):
                v_bias(tt)
            for s in range(NT + 2):
                if s < NT:
                    v_bias(NT + s)
                if 1 <= s <= NT:
                    dve.wait_ge(v_act, NT + s)
                    norm_stats(vn, s - 1, vln_stats)
                if s >= 2:
                    norm_apply(vn, s - 2, vln_std, s - 1, 3, vln_done)
            dve.wait_ge(vln_done, NT)
            for g in range(CH):
                dve.wait_ge(u_act, g + 1)
                dve.wait_ge(sp_mm, g + 1)
                pv = ps[:, g, :].rearrange("p (n q) -> p n q", n=NT)
                tmpv = gate_tmp[:, g % 2, :]
                step.done(nc.vector.tensor_tensor(tmpv.rearrange("p (n q) -> p n q", n=NT), pv,
                                                  bc(bs[:, g:g + 1, :], [P, NT, P]), ALU.add))
                step.wait()
                nc.vector.tensor_tensor(uT[:, g, :], uT[:, g, :], tmpv, ALU.mult).then_inc(uv_done, 1)
                dve.wait_ge(uv_done, g + 1)
            moe(1)
            for s in range(NT + 1):
                if s < NT:
                    sum_ready(1)(s)
                    norm_stats(xres, s, ln_stats)
                if s >= 1:
                    norm_apply(xres, s - 1, ln_std, 4 * NT + s, 5, ln_done)

        @block.gpsimd
        def _(pool):
            step = Steps(pool, pool_step)

            def moe(l):
                for tt in range(NT):
                    pool.wait_ge(perm_done, (2 * l + 1) * NT + tt + 1)
                    pool.dma_start(xs[l][tt * P:(tt + 1) * P, :], xperm[:, tt, :]).then_inc(xs_out, 16)
                pool.wait_ge(xs_out, 64 * (l + 1))
                pool.wait_ge(tr_done, (2 * l + 2) * 2 * NT)
                pool.wait_ge(counts_ready, l + 1)
                base = l * E

                def by_rows(n, move):
                    count = pool.value_load(cnt_tab[0:1, bass.ds(n, 1)], min_val=0, max_val=T)

                    def choose(steps):
                        if len(steps) == 1:
                            move(steps[0])
                            return
                        with pool.If(count > steps[1]):
                            move(steps[0])
                        with pool.Else():
                            choose(steps[1:])
                        pool.nop()

                    choose(ROW_STEPS)

                def gather(n, u, first, q):
                    if not first:
                        pool.wait_ge(scattered[u % 2], (n - u % 2) * 8 - 16 + 16 * (l * E // 2))
                        pool.wait_ge(xg_tr, n + (base - 3))
                    if u == 0:
                        pool.wait_ge(idx_done, q + (l * QUADS + 1))
                    pool.tensor_copy(idx_cur[0:NB, u:u + 1], idx_tab[0:NB, bass.ds(n, 1)]).then_inc(idx_cp, 1)
                    pool.wait_ge(idx_cp, n + (base + 1))
                    pool.sem_inc(pool_tick, 1)
                    by_rows(n, lambda rows: pool.indirect_dma_start(
                        out=xg[0:rows, u, :], out_offset=None, in_=xs[l],
                        in_offset=bass.IndirectOffsetOnAxis(ap=idx_cur[0:rows, u:u + 1], axis=0),
                        bounds_check=T - 1, oob_is_err=False).then_inc(gathered[u], 16))

                def scatter(n, u, first):
                    b = u % 2
                    pool.wait_ge(y_dve, n + (base + 1))
                    pool.wait_ge(y_act, n + (base + 1))
                    if not (first and u == 0):
                        pool.wait_ge(scattered[1 - b], (n - u) * 8 + (16 * ((u + 1) // 2) + 16 * (l * E // 2)))
                    pool.sem_inc(pool_tick, 1)
                    by_rows(n, lambda rows: pool.indirect_dma_start(
                        out=acc[l], out_offset=bass.IndirectOffsetOnAxis(ap=idx_cur[0:rows, u:u + 1], axis=0),
                        in_=ysb[0:rows, b, :], in_offset=None, bounds_check=T - 1, oob_is_err=False,
                        compute_op=ALU.add).then_inc(scattered[b], 16))

                gather(0, 0, True, 0)
                gather(1, 1, True, 0)
                for u in range(SLOTS):
                    gather(u + 2, (u + 2) % SLOTS, u < 2, (u + 2) // SLOTS)
                    scatter(u, u, True)
                with pool.Fori(1, QUADS - 1) as i:
                    for u in range(SLOTS):
                        gather(i * SLOTS + (u + 2), (u + 2) % SLOTS, False, i + (u + 2) // SLOTS)
                        scatter(i * SLOTS + u, u, False)
                for u in range(SLOTS):
                    if u < 2:
                        gather(E - SLOTS + u + 2, u + 2, False, QUADS - 1)
                    scatter(E - SLOTS + u, u, False)
                for b in range(2):
                    pool.wait_ge(scattered[b], 16 * (l + 1) * E // 2)
                overflow_pool(pool, l)
                pool.sem_inc(acc_ready, 1)
                pool.wait_ge(sh_y, 2 * NT * (l + 1))
                for tt in range(1, NT):
                    pool.wait_ge(acc_in[tt], 16 * (l + 1))
                    pool.tensor_tensor(xres[:, tt, :], xres[:, tt, :], xperm[:, tt, :], ALU.add).then_inc(acc_sum, 1)

            pool.dma_start(bconsts[:], t["bconsts"]).then_inc(bconst_in, 16)
            pool.memset(zeros[:], 0.0).then_inc(zero_set, 1)
            pool.wait_ge(zero_set, 1)
            pool.wait_ge(qkv_mm, 1)
            for l in range(DEPTH):
                for tt in range(NT):
                    pool.dma_start(acc[l][tt * P:(tt + 1) * P, :].rearrange("p (a c) -> p a c", a=4),
                                   zeros[:].unsqueeze(1).to_broadcast([P, 4, 256])).then_inc(acc_out, 16)
            pool.wait_ge(acc_out, 16 * DEPTH * NT)
            moe(0)
            moe(1)


def constants():
    p = np.arange(P)
    c = np.zeros((P, 128 + 512 + 64 + NB + 2), np.float32)
    c[:, 0:128] = np.eye(P)
    pos = np.arange(T)
    inv = 10000.0 ** (-np.arange(16) / 16.0)
    ang = np.stack([pos // GRID_W, pos % GRID_W], -1)[:, :, None].astype(np.float32) * inv.astype(np.float32)
    cos, sin = np.cos(ang.astype(np.float64)), np.sin(ang.astype(np.float64))
    rc = np.stack([cos, cos], 2).reshape(T, 64)
    rs = np.stack([-sin, sin], 2).reshape(T, 64)
    c[:, 128:384] = rc.reshape(NT, P, 64).transpose(1, 0, 2).reshape(P, -1)
    c[:, 384:640] = rs.reshape(NT, P, 64).transpose(1, 0, 2).reshape(P, -1)
    c[:, 640:704] = (np.arange(8)[None, :] < np.arange(8)[:, None]).reshape(1, 64)
    c[:, 704:704 + NB] = np.arange(NB)
    c[:, 704 + NB] = -p
    c[:, 705 + NB] = T + p
    b = np.zeros((P, 256 + 12), np.float32)
    b[:, 0:128] = p[:, None] < p[None, :]
    b[:, 128:256] = 1
    for tt in range(NT):
        b[:, 256 + 3 * tt] = P * tt - T
        b[:, 257 + 3 * tt] = p
        b[:, 258 + 3 * tt] = 1
    s = np.arange(T)
    a = 2 * np.pi * np.mod(np.outer(s, s), T) / T
    k = 2 * np.pi * np.mod(np.outer(p, p), P) / P
    d = np.zeros((P, 4352), np.float64)
    d[:, 0:2048] = np.cos(a).reshape(NT, P, T).transpose(1, 0, 2).reshape(P, -1)
    d[:, 2048:4096] = np.sin(a).reshape(NT, P, T).transpose(1, 0, 2).reshape(P, -1)
    d[:, 4096:4224] = np.cos(k) / math.sqrt(T * P)
    d[:, 4224:4352] = -np.sin(k) / math.sqrt(T * P)
    return {"consts": c, "bconsts": b, "dft": d.astype(np.float32)}


_INS = ["x", "ln_in_g", "ln_in_b", "e_w_in", "e_w_fourier", "e_q_gain", "e_k_gain", "e_w_out", "o_w_in", "o_b_in",
        "o_v_ln_g", "o_v_ln_b", "o_w_spatial", "o_b_spatial", "o_w_out", "ln_mix_g", "ln_mix_b", "ln_ffn_g", "ln_ffn_b",
        "router_w", "router_b", "exp_w_gate", "exp_w_up", "exp_w_down", "sh_w_gate", "sh_w_up", "sh_w_down"]


def kernel(**inputs):
    import concourse.bacc as _bacc
    from concourse.bass_utils import run_bass_kernel_spmd as _run

    nc = _bacc.Bacc("TRN2", target_bir_lowering=False, num_devices=1)
    arrays = {n: np.ascontiguousarray(inputs[n]) for n in _INS}
    arrays["u_bias"] = np.ascontiguousarray(arrays["o_b_in"][0, 0:D].reshape(CH, P).T)
    arrays.update(constants())
    t = {n: nc.dram_tensor(f"in_{n}", a.shape, mybir.dt.from_np(a.dtype), kind="ExternalInput").ap()
         for n, a in arrays.items()}
    out = nc.dram_tensor("out_x", [1, T, D], F32, kind="ExternalOutput").ap()
    build(nc, t, out)
    r = _run(nc, [{f"in_{n}": a for n, a in arrays.items()}], core_ids=[0])
    return r.results[0]["out_x"]
```

```python
import math

import numpy as np

import concourse.bass as bass
from concourse import mybir
from contextlib import ExitStack

F32 = mybir.dt.float32
BF16 = mybir.dt.bfloat16
F16 = mybir.dt.float16
I32 = mybir.dt.int32
ALU = mybir.AluOpType
ACT = mybir.ActivationFunctionType
AX = mybir.AxisListType.X

P = 128
D = 1024
T = 512
NT = T // P
NK = D // P
GRID_W = 64
N_FGROUPS = 4
N_HEADS = 8
HEAD_DIM = 64
PAIRS = N_HEADS // 2
F_WIDTH = 512
QKV_WIDTH = 768
QK_HEADS = 10
E_IN = F_WIDTH + QKV_WIDTH
CH = 8
E = 64
FE = 256
FC = FE // P
TOP_K = 8
N_EGROUPS = 8
TOPK_GROUPS = 4
ROUTE_SCALE = 2.5
LN_EPS = 1e-5
QK_EPS = 1e-6
ALPHA = 4.0 ** 0.25
DEPTH = 2

NB = 96
QUADS = E // 4
ROW_STEPS = (NB, 80, 64)
LEVELS = -(-T // NB)
BLOCKS = NB // 32
SLOTS = 4
SLOT = 3 * D * FE // P
PER_ITEM = 48
SHARED = {2: (0, 1), 3: (2,), 4: (3,), 5: (4,), 6: (5,), 7: (6, 7)}
IT_WIN, IT_DFT, IT_WOUT, IT_SH0 = 0, 2, 3, 5
IT_EXP = (6, 6 + E + 7)
IT_OWIN, IT_OWOUT, IT_SH1 = 6 + E, 6 + E + 4, 6 + E + 6
BIG = 1.0e30


def slot_of(item):
    return item % SLOTS


def full_value(item):
    return PER_ITEM * (item // SLOTS + 1)


def build(nc, t, out):
    with ExitStack() as ctx:
        def sb(name, shape, dt=F32):
            return ctx.enter_context(nc.sbuf_tensor(name, shape, dt))

        def sem(name):
            return ctx.enter_context(nc.semaphore(name))

        ring = sb("ring", [P, SLOTS, SLOT])
        xres = sb("xres", [P, NT, D])
        xperm = sb("xperm", [P, NT, D])
        xT = sb("xT", [P, NK, T])
        lnp = sb("lnp", [P, 2, D])
        consts = sb("consts", [P, 128 + 512 + 64 + NB + 2 + 33])
        ident = consts[:, 0:128]
        rope_c = consts[:, 128:384].rearrange("p (t d) -> p t d", t=NT)
        rope_s = consts[:, 384:640].rearrange("p (t d) -> p t d", t=NT)
        earlier = consts[:, 640:704].rearrange("p (i j) -> p i j", i=8)
        iota = consts[:, 704:704 + NB]
        negslot = consts[:, 704 + NB:705 + NB]
        dump = consts[:, 705 + NB:706 + NB]
        mine32 = consts[:, 706 + NB:738 + NB]
        quarter = consts[:, 738 + NB:739 + NB]
        bconsts = sb("bconsts", [P, 256 + 12], BF16)
        tok_all = sb("tok_all", [P, NT, P], F16)
        before = bconsts[:, 0:128]
        ones = bconsts[:, 128:256]
        posb = bconsts[:, 256:268].rearrange("p (t c) -> p t c", t=NT)
        work = sb("work", [P, 13000])
        zeros = work[:, 12864:12864 + P]

        def carve(*sizes):
            at, got = 0, []
            for n in sizes:
                got.append(work[:, at:at + n])
                at += n
            assert at <= 13000, at
            return got

        stats_w = work[:, 0:96]
        stats = stats_w[:, 0:48].rearrange("p (t h s) -> p t h s", t=NT, h=2)
        mv = stats_w[:, 48:56].rearrange("p (t s) -> p t s", t=NT)
        vare = stats_w[:, 56:60]
        std = stats_w[:, 60:64]
        rstd = stats_w[:, 64:68]

        _, qkv_w, rot_w, qkT_w, aT_w, fw_w, gain_w, sm_w, tmp_w = carve(
            96, NT * QKV_WIDTH, NT * 640, 5 * T, 4 * T, 1024, 128, 96, 1280)
        qkv = qkv_w.rearrange("p (t c) -> p t c", t=NT)
        rot = rot_w.rearrange("p (t c) -> p t c", t=NT)
        attn = rot_w[:, 0:NT * 512].rearrange("p (t c) -> p t c", t=NT)
        qkT = qkT_w.rearrange("p (i t) -> p i t", i=5)
        aT = aT_w.rearrange("p (g t) -> p g t", g=4)
        probs = aT_w[:, 0:1024].rearrange("p (b k) -> p b k", b=2)
        probsT = aT_w[:, 1024:2048].rearrange("p (b c q) -> p b c q", b=2, c=4)
        fw = fw_w.rearrange("p (g s d) -> p g s d", g=4, s=2)
        odd_sums = tmp_w[:, 0:768].rearrange("p (b s) -> p b s", b=3)
        tmp1, tmp2 = tmp_w[:, 0:640], tmp_w[:, 640:1280]
        gains = gain_w.rearrange("p (a d) -> p a d", a=2)
        qk_ss, qk_rs = sm_w[:, 0:40], sm_w[:, 40:80]
        nmax, rsum, rinv = sm_w[:, 80:82], sm_w[:, 82:86], sm_w[:, 86:88]
        zmix = xperm[:].rearrange("p t (g s d) -> p t g s d", g=4, s=2)
        catT = xT

        _, uT_w, v_w, ws_w, wsT_w, bv_w, bs_w, bu_w = carve(96, CH * T, NT * D, D, D, D, D, CH)
        uT = uT_w.rearrange("p (g t) -> p g t", g=CH)
        vn = v_w.rearrange("p (t c) -> p t c", t=NT)
        ws = ws_w.rearrange("p (g q) -> p g q", g=CH)
        wsT = wsT_w.rearrange("p (g q) -> p g q", g=CH)
        bs = bs_w.rearrange("p (g q) -> p g q", g=CH)
        bu_col = bu_w
        gate_tmp = ws_w.rearrange("p (b t) -> p b t", b=2)

        router = work[:, 12424:12424 + NK * E].rearrange("p (j e) -> p j e", j=NK)
        rb_w = work[:, 12936:12936 + E]
        (_, sc_w, sel_w, selm_w, rep_w, m8_w, g_w, cmp_w, rank_w, mask_w, tab_w, pe_w, pi_w,
         ix_w, ix4_w, place_w, sh_w, xgT_w, sil_w, h_w, y_w) = carve(
            96, NT * E, NT * E, NT * E, NT * E, 256 + 32, 160, 3 * 256, NT * E, NT * E // 2,
            NT * E * 3, 4 * NT * NB // 2, 24 + 8, 4 * E + 16, BLOCKS * (E + 8), 4 * NB, 2 * D, 2 * NK * NB, 2 * FC * NB, 2 * FC * NB, 2 * D)
        scores, sel, selm, rep = (w.rearrange("p (t e) -> p t e", t=NT) for w in (sc_w, sel_w, selm_w, rep_w))
        m8 = m8_w[:, 0:256].rearrange("p (t g k) -> p t g k", t=NT, g=N_EGROUPS)
        v8 = m8_w[:, 256:288].rearrange("p (t k) -> p t k", t=NT)
        gsc, grank, gmask, gpen = (g_w[:, 32 * i:32 * i + 32].rearrange("p (t g) -> p t g", t=NT) for i in range(4))
        wsum, wfac = g_w[:, 128:132], g_w[:, 132:136]
        cmps = [cmp_w[:, 256 * i:256 * i + 256].rearrange("p (t i j) -> p t i j", t=NT, i=8) for i in range(3)]
        rankm = rank_w.rearrange("p (t e) -> p t e", t=NT)
        maskb = mask_w.bitcast(BF16).rearrange("p (t e) -> p t e", t=NT)
        tab = tab_w.bitcast(BF16).rearrange("p (t e c) -> p t e c", t=NT, e=E)
        pick = pe_w.bitcast(BF16).rearrange("p (b t s) -> p b t s", b=4, t=NT)
        pi = pi_w[:, 0:24].rearrange("p (e c) -> p e c", e=4)
        pi_idx, pi_wt = pi_w[:, 24:28], pi_w[:, 28:32]
        idx_f, w_slot = ix_w[:, 0:E], ix_w[:, E:2 * E]
        idx_tab = ix_w[:, 2 * E:3 * E].bitcast(I32)
        cnt_tab = ix_w[:, 3 * E:4 * E].bitcast(I32)
        cnt_max = ix_w[:, 4 * E:4 * E + 1].bitcast(I32)
        idx_cur = ix_w[:, 4 * E + 4:4 * E + 8].bitcast(I32)
        of_idx = ix_w[:, 4 * E + 8:4 * E + 9].bitcast(I32)
        of_f, of_w1, of_w2, of_wt = (ix_w[:, 4 * E + 9 + i:4 * E + 10 + i] for i in range(4))
        idx4_tab = ix4_w[:, 0:BLOCKS * E].bitcast(I32)
        idx4_cur = ix4_w[:, BLOCKS * E:BLOCKS * (E + 4)].bitcast(I32)
        idx4_f = ix4_w[:, BLOCKS * (E + 4):BLOCKS * (E + 8)]
        place = place_w.rearrange("p (a s) -> p a s", s=32)
        xg = xperm[:].rearrange("p t d -> p (t d)")[:, 0:4 * 8 * NB].rearrange("p (b k c) -> p b k c", b=4, c=256)
        of_xg, of_rows = xperm[:, 0, :], xperm[:, 1, :]
        xT_w = xT[:].rearrange("p j t -> p (j t)")
        sh_down = xT_w[:, 0:2048].rearrange("p (c d) -> p c d", c=FC)
        xgT = xgT_w.rearrange("p (b j s) -> p b j s", b=2, j=NK)
        sil = sil_w.rearrange("p (b c s) -> p b c s", b=2, c=FC)
        hT = h_w.rearrange("p (b c s) -> p b c s", b=2, c=FC)
        ysb = y_w.rearrange("p (b d) -> p b d", b=2)
        sh_sil = sh_w[:, 0:FC * T].rearrange("p (c t) -> p c t", c=FC)
        sh_h = sh_w[:, FC * T:2 * FC * T].rearrange("p (c t) -> p c t", c=FC)
        of_gate = xT_w[:, 0:2048].rearrange("p (j f) -> p j f", j=NK)
        of_up = xT_w[:, 2048:4096].rearrange("p (j f) -> p j f", j=NK)
        of_down = xperm[:, 2:4, :]

        ps = ctx.enter_context(nc.psum_tensor("ps", [P, 8, 512], F32))

        xs = [nc.dram_tensor(f"tokens{l}", [T, D], F32).ap() for l in range(DEPTH)]
        acc = [nc.dram_tensor(f"sum{l}", [T + NB, D], F32).ap() for l in range(DEPTH)]

        def rings(item, lo, hi):
            return ring[:, slot_of(item), lo:hi]

        def win(j):
            it = IT_WIN + j // 4
            return rings(it, (j % 4) * E_IN, (j % 4 + 1) * E_IN)

        dft_c = rings(IT_DFT, 0, 1024).rearrange("p (t s) -> p t s", t=NT)
        dft_s = rings(IT_DFT, 1024, 2048).rearrange("p (t s) -> p t s", t=NT)
        chn_c = rings(IT_DFT, 2048, 2176)
        chn_s = rings(IT_DFT, 2176, 2304)
        wfour = rings(IT_DFT, 2304, 2816)

        def wout(first, i):
            return rings(first + i // 4, (i % 4) * D, (i % 4 + 1) * D)

        def owin(n):
            return rings(IT_OWIN + n, 0, 4096).rearrange("p (j c) -> p j c", j=NK)

        def expert(slot):
            w = ring[:, slot, :]
            return (w[:, 0:2048].rearrange("p (j f) -> p j f", j=NK),
                    w[:, 2048:4096].rearrange("p (j f) -> p j f", j=NK),
                    w[:, 4096:6144].rearrange("p (c d) -> p c d", c=FC))

        x_in, const_in, bconst_in = [sem(f"x_in{tt}") for tt in range(NT)], sem("const_in"), sem("bconst_in")
        slot_full = [sem(f"slot_full{s}") for s in range(SLOTS)]
        lnp_in, small_in = sem("lnp_in"), sem("small_in")
        ln_stats, ln_std, ln_done = sem("ln_stats"), sem("ln_std"), sem("ln_done")
        perm_done = sem("perm_done")
        tr_done, xT_dve, xT_act = sem("tr_done"), sem("xT_dve"), sem("xT_act")
        dve_step, pool_step = sem("dve_step"), sem("pool_step")
        sp_tick, dve_tick, pool_tick = sem("sp_tick"), sem("dve_tick"), sem("pool_tick")
        aT_mm, aT_cp, qkv_mm, qkv_cp = sem("aT_mm"), sem("aT_cp"), sem("qkv_mm"), sem("qkv_cp")
        fw_mm, fw_cp, z_mm, z_cp = sem("fw_mm"), sem("fw_cp"), sem("z_mm"), sem("z_cp")
        four_mm, four_cp, odd_cp = sem("four_mm"), sem("four_cp"), sem("odd_cp")
        qk_ssq, qk_root, rot_done, qkT_tr, qkT_cp = (sem(n) for n in ("qk_ssq", "qk_root", "rot_done", "qkT_tr", "qkT_cp"))
        s_mm, max_done, p_done, pT_tr, pT_cp = (sem(n) for n in ("s_mm", "max_done", "p_done", "pT_tr", "pT_cp"))
        o_mm, rinv_done, o_cp, atT_tr, atT_cp = (sem(n) for n in ("o_mm", "rinv_done", "o_cp", "atT_tr", "atT_cp"))
        wout_mm, resid_done = sem("wout_mm"), sem("resid_done")
        wsT_tr, wsT_cp, v_mm, v_pre, v_act = (sem(n) for n in ("wsT_tr", "wsT_cp", "v_mm", "v_pre", "v_act"))
        vln_stats, vln_std, vln_done = (sem(n) for n in ("vln_stats", "vln_std", "vln_done"))
        u_mm, u_act, sp_mm, uv_done = (sem(n) for n in ("u_mm", "u_act", "sp_mm", "uv_done"))
        xs_out, zero_set, acc_out = sem("xs_out"), sem("zero_set"), sem("acc_out")
        lg_mm, sg_done, mask_done, rk_mm, tab_done, counts_ready = (
            sem(n) for n in ("lg_mm", "sg_done", "mask_done", "rk_mm", "tab_done", "counts_ready"))
        shg_mm, sh_silu, sh_mul, shd_mm, sh_y = (sem(n) for n in ("shg_mm", "sh_silu", "sh_mul", "shd_mm", "sh_y"))
        router_in, sh_down_in = sem("router_in"), sem("sh_down_in")
        place_mm, placed = sem("place_mm"), sem("placed")
        pick_done, pick_mm, pi_cp, pi_mid, idx_done, idx_cp = (
            sem(n) for n in ("pick_done", "pick_mm", "pi_cp", "pi_mid", "idx_done", "idx_cp"))
        gathered = [sem(f"gathered{b}") for b in range(4)]
        scattered = [sem(f"scattered{b}") for b in range(2)]
        xgT_done = sem("xgT_done")
        gate_mm, up_mm, silu_done, h_done = sem("gate_mm"), sem("up_mm"), sem("silu_done"), sem("h_done")
        down_mm, y_dve, y_act = sem("down_mm"), sem("y_dve"), sem("y_act")
        counts_read = sem("counts_read")
        acc_ready, acc_in, acc_sum = sem("acc_ready"), [sem(f"acc_in{tt}") for tt in range(NT)], sem("acc_sum")
        first_sum = sem("first_sum")
        OF = ["of_w", "of_pick", "of_pi", "of_ix", "of_gat", "of_pm", "of_tr", "of_xt", "of_gu", "of_si", "of_h", "of_dn", "of_y", "of_sc", "of_gat_dma", "of_sc_dma", "of_level"]
        of = [{n: sem(f"{n}{l}") for n in OF} for l in range(DEPTH)]
        out_done = sem("out_done")
        block = ctx.enter_context(nc.Block())

        class Steps:

            def __init__(self, eng, s):
                self.eng, self.s, self.n = eng, s, 0

            def done(self, ins):
                self.n += 1
                ins.then_inc(self.s, 1)

            def wait(self):
                self.eng.wait_ge(self.s, self.n)

        def overflow(eng, l, produced, body, level=None):
            s = of[l]
            eng.wait_ge(counts_ready, l + 1)
            most = eng.value_load(cnt_max[0:1, 0:1], min_val=0, max_val=T)
            with eng.If(most > NB):
                with eng.Fori(1, LEVELS) as b:
                    with eng.If(most > b * NB):
                        if level is not None:
                            level(b)
                        with eng.Fori(0, E) as e:
                            count = eng.value_load(cnt_tab[0:1, bass.ds(e, 1)], min_val=0, max_val=T)
                            with eng.If(count > b * NB):
                                body(s, e, b * E + e - E)
                            with eng.Else():
                                eng.drain()
                                for name, by in produced:
                                    eng.sem_inc(s[name], by)
                            eng.nop()
                    eng.nop()
            eng.nop()

        def overflow_sp(sp, l):
            def body(s, e, q):
                with sp.If(q > 0):
                    sp.wait_ge(s["of_sc"], q)
                    sp.sem_inc(sp_tick, 1)
                sp.nop()
                for dst, name in ((of_gate, "exp_w_gate"), (of_up, "exp_w_up")):
                    sp.dma_start(dst, t[name][l, bass.ds(e, 1), :, :].rearrange("a (p j) f -> p (a j) f", j=NK))\
                        .then_inc(s["of_w"], 16)
                sp.dma_start(of_down, t["exp_w_down"][l, bass.ds(e, 1), :, :].rearrange("a (p c) d -> p (a c) d", c=FC))\
                    .then_inc(s["of_w"], 16)
                sp.wait_ge(s["of_w"], q * 48 + 48)
                sp.sem_inc(sp_tick, 1)

            sp.wait_ge(down_mm, (l + 1) * E)
            overflow(sp, l, [("of_w", 48)], body)

        def overflow_pe(pe, l):
            def body(s, e, q):
                pe.wait_ge(s["of_pick"], q + 1)
                for tt in range(NT):
                    ins = mm(ps[0:NB, 7, 0:6], pick[:, 0, tt, :],
                             tab[:, tt, bass.ds(e, 1), :].rearrange("p a c -> p (a c)"), tt == 0, tt == NT - 1)
                ins.then_inc(s["of_pi"], 1)
                pe.wait_ge(s["of_pm"], q + 1)
                for j in range(NK):
                    ins = nc.tensor.transpose(ps[:, j // 4, (j % 4) * NB:(j % 4 + 1) * NB],
                                              of_rows[0:NB, j * P:(j + 1) * P], ident[0:NB, 0:NB])
                ins.then_inc(s["of_tr"], 1)
                pe.wait_ge(s["of_xt"], q + 1)
                pe.wait_ge(s["of_w"], q * 48 + 48)
                for w, bank in ((of_gate, 2), (of_up, 3)):
                    for c in range(FC):
                        for j in range(NK):
                            ins = mm(ps[:, bank, c * NB:(c + 1) * NB], w[:, j, c::FC], xgT[:, 0, j, :],
                                     j == 0, j == NK - 1)
                ins.then_inc(s["of_gu"], 1)
                pe.wait_ge(s["of_h"], q + 1)
                for hf in range(2):
                    for c in range(FC):
                        ins = mm(ps[0:NB, 4 + hf, :], hT[:, 0, c, :], of_down[:, c, hf * 512:(hf + 1) * 512],
                                 c == 0, c == FC - 1)
                ins.then_inc(s["of_dn"], 1)

            pe.wait_ge(y_dve, (l + 1) * E)
            pe.wait_ge(y_act, (l + 1) * E)
            overflow(pe, l, [("of_pi", 1), ("of_tr", 1), ("of_gu", 1), ("of_dn", 1)], body)

        def overflow_act(act, l):
            def body(s, e, q):
                act.wait_ge(s["of_gat"], q + 1)
                nc.scalar.activation(of_rows[0:NB, :].rearrange("q (j a f) -> q j a f", a=4, j=NK),
                                     of_xg[0:NB, :].rearrange("q (a j f) -> q j a f", a=4, j=NK), ACT.Copy)\
                    .then_inc(s["of_pm"], 1)
                act.wait_ge(s["of_gu"], q + 1)
                nc.scalar.activation(sil[:, 0, :, :], ps[:, 2, 0:FC * NB].rearrange("p (c s) -> p c s", c=FC), ACT.Silu)\
                    .then_inc(s["of_si"], 1)

            overflow(act, l, [("of_pm", 1), ("of_si", 1)], body)

        def overflow_dve(dve, step, l):
            s = of[l]

            def level(b):
                nc.vector.tensor_scalar(rankm, rankm, float(NB), None, ALU.subtract).then_inc(s["of_level"], 1)
                dve.wait_ge(s["of_level"], b)
                dve.sem_inc(dve_tick, 1)

            def body(s, e, q):
                with dve.If(q > 0):
                    dve.wait_ge(s["of_sc"], q)
                    dve.sem_inc(dve_tick, 1)
                dve.nop()
                nc.vector.tensor_tensor(pick[:, 0, :, :], rankm[:, :, bass.ds(e, 1)].to_broadcast([P, NT, NB]),
                                        iota.unsqueeze(1).to_broadcast([P, NT, NB]), ALU.is_equal).then_inc(s["of_pick"], 1)
                dve.wait_ge(s["of_pi"], q + 1)
                nc.vector.tensor_copy(pi_w[0:NB, 0:6], ps[0:NB, 7, 0:6]).then_inc(s["of_ix"], 1)
                dve.wait_ge(s["of_ix"], q * 4 + 1)
                nc.vector.scalar_tensor_tensor(of_f[0:NB, :], pi_w[0:NB, 2:3], negslot[0:NB, :], pi_w[0:NB, 0:1],
                                               ALU.mult, ALU.add)
                nc.vector.tensor_tensor(of_w1[0:NB, :], pi_w[0:NB, 3:4], pi_w[0:NB, 4:5], ALU.add).then_inc(s["of_ix"], 1)
                dve.wait_ge(s["of_ix"], q * 4 + 2)
                nc.vector.tensor_tensor(of_wt[0:NB, :], of_w1[0:NB, :], pi_w[0:NB, 5:6], ALU.add).then_inc(s["of_ix"], 1)
                nc.vector.scalar_tensor_tensor(of_idx[0:NB, :], of_f[0:NB, :], dump[0:NB, :], pi_w[0:NB, 1:2],
                                               ALU.add, ALU.add).then_inc(s["of_ix"], 1)
                dve.wait_ge(s["of_tr"], q + 1)
                nc.vector.tensor_copy(xgT[:, 0, :, :].rearrange("p (a k) s -> p a (k s)", a=2), ps[:, 0:2, 0:4 * NB])\
                    .then_inc(s["of_xt"], 1)
                dve.wait_ge(s["of_si"], q + 1)
                nc.vector.tensor_tensor(hT[:, 0, :, :], sil[:, 0, :, :],
                                        ps[:, 3, 0:FC * NB].rearrange("p (c s) -> p c s", c=FC), ALU.mult)\
                    .then_inc(s["of_h"], 1)
                dve.wait_ge(s["of_dn"], q + 1)
                dve.wait_ge(s["of_ix"], q * 4 + 4)
                nc.vector.tensor_scalar(ysb[0:NB, 0, :], ps[0:NB, 4:6, :].rearrange("p b c -> p (b c)"), of_wt[0:NB, :],
                                        None, ALU.mult).then_inc(s["of_y"], 1)

            for b in range(2):
                dve.wait_ge(scattered[b], 16 * (l + 1) * E // 2)
            dve.wait_ge(y_dve, (l + 1) * E)
            overflow(dve, l, [("of_pick", 1), ("of_ix", 4), ("of_xt", 1), ("of_h", 1), ("of_y", 1)], body, level)

        def overflow_pool(pool, l):
            landed = pool.alloc_register(f"of_landed{l}")
            pool.reg_mov(landed, 0)

            def body(s, e, q):
                pool.reg_add(landed, landed, 16)
                dma_count = pool.snap(landed)
                pool.wait_ge(s["of_ix"], q * 4 + 4)
                pool.sem_inc(pool_tick, 1)
                pool.indirect_dma_start(out=of_xg[0:NB, :], out_offset=None, in_=xs[l],
                                        in_offset=bass.IndirectOffsetOnAxis(ap=of_idx[0:NB, :], axis=0),
                                        bounds_check=T - 1, oob_is_err=False).then_inc(s["of_gat_dma"], 16)
                pool.wait_ge(s["of_gat_dma"], dma_count)
                pool.sem_inc(s["of_gat"], 1)
                pool.wait_ge(s["of_y"], q + 1)
                pool.sem_inc(pool_tick, 1)
                pool.indirect_dma_start(out=acc[l], out_offset=bass.IndirectOffsetOnAxis(ap=of_idx[0:NB, :], axis=0),
                                        in_=ysb[0:NB, 0, :], in_offset=None, bounds_check=T + NB - 1, oob_is_err=True,
                                        compute_op=ALU.add).then_inc(s["of_sc_dma"], 16)
                pool.wait_ge(s["of_sc_dma"], dma_count)
                pool.sem_inc(s["of_sc"], 1)

            overflow(pool, l, [("of_gat", 1), ("of_sc", 1)], body)

        @block.sync
        def _(sp):
            def load3(item, parts):
                s = slot_full[slot_of(item)]
                for dst, src in parts:
                    sp.dma_start(dst, src).then_inc(s, 16)

            def load_x(tt):
                sp.dma_start(xres[:, tt, :], t["x"][0, tt * P:(tt + 1) * P, :]).then_inc(x_in[tt], 16)

            def load_win(it):
                w = t["e_w_in"][0].rearrange("(p j) c -> p j c", j=NK)
                load3(IT_WIN + it, [(rings(IT_WIN + it, a * E_IN, b * E_IN).rearrange("p (j c) -> p j c", c=E_IN),
                                     w[:, 4 * it + a:4 * it + b, :]) for a, b in ((0, 2), (2, 3), (3, 4))])

            load_x(0)
            for a, name in enumerate(("ln_in_g", "ln_in_b")):
                sp.dma_start(lnp[:, a, :], t[name].partition_broadcast(P)).then_inc(lnp_in, 16)
            load_x(1)
            load_win(0)
            load_x(2)
            load_x(3)
            load_win(1)
            load3(IT_DFT, [(rings(IT_DFT, 0, 1024), t["dft"][:, 0:1024]),
                           (rings(IT_DFT, 1024, 2304), t["dft"][:, 1024:2304]),
                           (wfour.rearrange("p (g d) -> p g d", g=4), t["e_w_fourier"][0].rearrange("g c d -> c g d"))])

            def load_wout(first, name, half):
                w = t[name][0].rearrange("(i p) c -> p i c", p=P)
                it = first + half
                load3(it, [(rings(it, a * D, b * D).rearrange("p (i c) -> p i c", c=D), w[:, 4 * half + a:4 * half + b, :])
                           for a, b in ((0, 2), (2, 3), (3, 4))])

            load_wout(IT_WOUT, "e_w_out", 0)
            sp.wait_ge(aT_mm, 4)
            load_wout(IT_WOUT, "e_w_out", 1)

            def load_shared(item, l):
                g, u, _ = expert(slot_of(item))
                up = t["sh_w_up"][l].rearrange("(p j) f -> p j f", j=NK)
                load3(item, [(g, t["sh_w_gate"][l].rearrange("(p j) f -> p j f", j=NK)),
                             (u[:, 0:4, :], up[:, 0:4, :]), (u[:, 4:8, :], up[:, 4:8, :])])

            load_shared(IT_SH0, 0)

            def load_expert(l, e, slot):
                g, u, d = expert(slot)
                for dst, name in ((g, "exp_w_gate"), (u, "exp_w_up")):
                    sp.dma_start(dst, t[name][l, bass.ds(e, 1), :, :].rearrange("a (p j) f -> p (a j) f", j=NK))\
                        .then_inc(slot_full[slot], 16)
                sp.dma_start(d, t["exp_w_down"][l, bass.ds(e, 1), :, :].rearrange("a (p c) d -> p (a c) d", c=FC))\
                    .then_inc(slot_full[slot], 16)

            def load_experts(l, frees):
                for u in range(SLOTS):
                    sp.wait_ge(*frees[u])
                    if u == SLOTS - 1:
                        sp.wait_ge(gathered[1], 16 * BLOCKS * (l * E // 4 + 1))
                    load_expert(l, u, slot_of(IT_EXP[l] + u))
                with sp.Fori(1, E // SLOTS) as i:
                    for u in range(SLOTS):
                        sp.wait_ge(down_mm, i * SLOTS + (l * E + u - SLOTS + 1))
                        load_expert(l, i * SLOTS + u, slot_of(IT_EXP[l] + u))

            load_experts(0, [(four_mm, 4), (wout_mm, NT), (wout_mm, NT), (shg_mm, 4)])

            def load_owin(n):
                w, col, dst = t["o_w_in"][0].rearrange("(p j) c -> p j c", j=NK), (1024, 1536, 0, 512)[n], owin(n)
                load3(IT_OWIN + n, [(dst[:, a:b, :], w[:, a:b, col:col + 512]) for a, b in ((0, 3), (3, 6), (6, 8))])

            for n in range(3):
                sp.wait_ge(down_mm, E - SLOTS + 1 + n)
                load_owin(n)
            overflow_sp(sp, 0)
            sp.sem_inc(counts_read, 1)
            sp.wait_ge(acc_in[NT - 1], 16)
            load_owin(3)
            sp.wait_ge(v_mm, NT)
            load_wout(IT_OWOUT, "o_w_out", 0)
            sp.wait_ge(v_mm, 2 * NT)
            load_wout(IT_OWOUT, "o_w_out", 1)
            sp.wait_ge(u_mm, 4)
            load_shared(IT_SH1, 1)
            load_experts(1, [(u_mm, 8), (wout_mm, 2 * NT), (wout_mm, 2 * NT), (shg_mm, 8)])
            overflow_sp(sp, 1)
            for tt in range(NT):
                sp.wait_ge(ln_done, 4 * NT + tt + 1)
                sp.dma_start(out[0, tt * P:(tt + 1) * P, :], xres[:, tt, :]).then_inc(out_done, 16)
            sp.wait_ge(out_done, 16 * NT)

        def mm(o, lhsT, rhs, first, last):
            return nc.tensor.matmul(o, lhsT, rhs, start=first, stop=last)

        @block.tensor
        def _(pe):
            def arrived(item):
                pe.wait_ge(slot_full[slot_of(item)], full_value(item))

            def transpose_x(r, tt):
                pe.wait_ge(ln_done, r * NT + tt + 1)
                for hf in range(2):
                    if tt >= 2:
                        pe.wait_ge(xT_act if hf else xT_dve, r * NT + tt - 1)
                    for k in range(4):
                        j = 4 * hf + k
                        ins = nc.tensor.transpose(ps[:, 4 + (2 * tt + hf) % 4, k * P:(k + 1) * P],
                                                  xres[:, tt, j::NK], ident)
                    ins.then_inc(tr_done, 1)

            def xT_ready(r, tt=NT - 1):
                pe.wait_ge(xT_dve, r * NT + tt + 1)
                pe.wait_ge(xT_act, r * NT + tt + 1)

            def out_projection(r, first, ready):
                src = catT if r == 0 else uT
                for tt in range(NT):
                    if tt >= 2:
                        pe.wait_ge(resid_done, r * NT + tt - 1)
                    for hf in range(2):
                        for i in range(8):
                            ready(tt, hf, i)
                            ins = mm(ps[:, 2 * (tt % 2) + hf, :], src[:, i, tt * P:(tt + 1) * P],
                                     wout(first, i)[:, hf * 512:(hf + 1) * 512], i == 0, i == 7)
                    ins.then_inc(wout_mm, 1)
                    if tt >= 1:
                        transpose_x(2 * r + 1, tt - 1)

            def moe(l):
                r = 2 * l + 1

                def logits(tt):
                    xT_ready(r, tt)
                    for j in range(NK):
                        ins = mm(ps[:, 0, tt * E:(tt + 1) * E], xT[:, j, tt * P:(tt + 1) * P], router[:, j, :],
                                 j == 0, j == NK - 1)
                    return ins

                g, u, _ = expert(slot_of(IT_SH0 if l == 0 else IT_SH1))

                def shared_in(w, c, bank, lo=0, hi=T):
                    for j in range(NK):
                        ins = mm(ps[:, bank, lo:hi], w[:, j, c::FC], xT[:, j, lo:hi], j == 0, j == NK - 1)
                    return ins

                pe.wait_ge(router_in, 32 * (l + 1))
                pe.wait_ge(resid_done, l * NT + 3)
                for tt in range(NT - 1):
                    logits(tt)
                arrived(IT_SH0 if l == 0 else IT_SH1)
                shared_in(g, 0, 1, 0, 3 * P)
                transpose_x(r, NT - 1)
                logits(NT - 1).then_inc(lg_mm, 1)
                shared_in(g, 0, 1, 3 * P, T).then_inc(shg_mm, 1)
                pe.wait_ge(resid_done, (l + 1) * NT)
                shared_in(g, 1, 2).then_inc(shg_mm, 1)
                pe.wait_ge(bconst_in, 32)
                pe.wait_ge(mask_done, l + 1)
                for tt in range(NT):
                    for t2 in range(tt + 1):
                        mm(ps[:, 5, tt * E:(tt + 1) * E], before if t2 == tt else ones, maskb[:, t2, :],
                           t2 == 0, t2 == tt)
                for tt in range(NT):
                    ins = mm(ps[:, 5, NT * E:(NT + 1) * E], ones, maskb[:, tt, :], tt == 0, tt == NT - 1)
                ins.then_inc(rk_mm, 1)
                shared_in(u, 0, 4).then_inc(shg_mm, 1)

                def slot_table(q):
                    if not (isinstance(q, int) and q == 0):
                        pe.wait_ge(idx_done, q + l * E // 4)
                    for b in range(4):
                        pe.wait_ge(pick_done, q * 4 + (l * E + b + 1))
                        for tt in range(NT):
                            ins = mm(ps[0:NB, 7, 6 * b:6 * b + 6], pick[:, b, tt, :],
                                     tab[:, tt, bass.ds(q * 4 + b, 1), :].rearrange("p a c -> p (a c)"),
                                     tt == 0, tt == NT - 1)
                        ins.then_inc(pick_mm, 1)
                    for tt in range(NT):
                        ins = mm(ps[:, 7, 24:24 + 4 * NB], tok_all[:, tt, :], pick[:, :, tt, :], tt == 0, tt == NT - 1)
                    ins.then_inc(place_mm, 1)

                pe.wait_ge(tab_done, l + 1)
                slot_table(0)
                shared_in(u, 1, 6).then_inc(shg_mm, 1)
                base = l * E

                def shared_down(n):
                    pe.wait_ge(sh_down_in, 16 * (l + 1))
                    if n >= 2:
                        pe.wait_ge(sh_y, l * 2 * NT + n - 1)
                    for c in range(FC):
                        ins = mm(ps[:, 1 if n % 2 else 6, :], sh_h[:, c, (n // 2) * P:(n // 2 + 1) * P],
                                 sh_down[:, c, (n % 2) * 512:(n % 2 + 1) * 512], c == 0, c == FC - 1)
                    ins.then_inc(shd_mm, 1)

                def gate_or_up(n, u, up):
                    w, bank, done = expert(slot_of(IT_EXP[l] + u))[up], 2 + up, (gate_mm, up_mm)[up]
                    for c in range(FC):
                        for j in range(NK):
                            ins = mm(ps[:, bank, c * NB:(c + 1) * NB], w[:, j, c::FC], xgT[:, u % 2, j, :],
                                     j == 0, j == NK - 1)
                    ins.then_inc(done, 1)

                def down(n, u, first):
                    d = expert(slot_of(IT_EXP[l] + u))[2]
                    pe.wait_ge(h_done, n + (base + 1))
                    if not first:
                        pe.wait_ge(y_dve, n + base)
                        pe.wait_ge(y_act, n + base)
                    for hf in range(2):
                        for c in range(FC):
                            ins = mm(ps[0:NB, 4 + hf, :], hT[:, u % 2, c, :], d[:, c, hf * 512:(hf + 1) * 512],
                                     c == 0, c == FC - 1)
                    ins.then_inc(down_mm, 1)

                def expert_step(n, u, first=False, second=False, shared=()):
                    slot = slot_of(IT_EXP[l] + u)
                    pe.wait_ge(slot_full[slot], (n - u) * (PER_ITEM // SLOTS) + full_value(IT_EXP[l] + u))
                    pe.wait_ge(xgT_done, n + (base + 1))
                    if not first:
                        pe.wait_ge(silu_done, n + base)
                    gate_or_up(n, u, 0)
                    for k in shared:
                        shared_down(k)
                    if not first:
                        down(n - 1, (u - 1) % SLOTS, second)
                    gate_or_up(n, u, 1)

                slot_table(1)
                pe.wait_ge(sh_silu, 2 * (l + 1))
                pe.wait_ge(counts_ready, l + 1)
                pe.wait_ge(sh_mul, 2 * (l + 1))
                for n in range(2 * SLOTS):
                    if n == SLOTS:
                        slot_table(2)
                    expert_step(n, n % SLOTS, n == 0, n == 1, SHARED.get(n, ()))
                with pe.Fori(2, QUADS - 1) as q:
                    slot_table(q + 1)
                    for u in range(SLOTS):
                        expert_step(q * SLOTS + u, u)
                for u in range(SLOTS):
                    expert_step(E - SLOTS + u, u)
                down(E - 1, SLOTS - 1, False)
                overflow_pe(pe, l)

            pe.wait_ge(const_in, 16)
            def qkv_half(tt, half):
                for bank, lo, hi in ((0, 512, 1024), (1, 1024, 1280)):
                    for j in range(4 * half, 4 * half + 4):
                        ins = mm(ps[:, 2 * tt + bank, 0:hi - lo], xT[:, j, tt * P:(tt + 1) * P],
                                 win(j)[:, lo:hi], j == 0, j == NK - 1)
                return ins

            transpose_x(0, 0)
            transpose_x(0, 1)
            arrived(IT_WIN)
            for tt in range(NT):
                xT_ready(0, tt)
                qkv_half(tt, 0)
                if tt < 2:
                    transpose_x(0, tt + 2)
            arrived(IT_WIN + 1)
            for tt in range(NT):
                qkv_half(tt, 1).then_inc(qkv_mm, 1)
            pe.wait_ge(qkv_cp, 2)
            for g in range(4):
                for j in range(NK):
                    ins = mm(ps[:, g, :], win(j)[:, g * P:(g + 1) * P], xT[:, j, :], j == 0, j == NK - 1)
                ins.then_inc(aT_mm, 1)
                if g == 2:
                    arrived(IT_DFT)
                    pe.wait_ge(qkv_cp, NT)
                    mm(ps[:, 4, :], chn_c, wfour, True, True)
                    mm(ps[:, 5, :], chn_s, wfour, True, True).then_inc(fw_mm, 1)
            pe.wait_ge(fw_cp, 2)
            for tt in range(NT):
                if tt >= 2:
                    pe.wait_ge(z_cp, tt - 1)
                for g in range(4):
                    if tt == 0:
                        pe.wait_ge(aT_cp, g + 1)
                    ins = mm(ps[:, 6 - 2 * (tt % 2) + g // 2, (g % 2) * 256:(g % 2 + 1) * 256],
                             aT[:, g, 2 * P * (tt % 2) + tt // 2:2 * P * (tt % 2 + 1):2], fw[:, g, :, :].rearrange("p s d -> p (s d)"), True, True)
                ins.then_inc(z_mm, 1)

            def positions(g):
                bank = (0, 1, 3, 7)[g]
                for tt in range(NT):
                    pe.wait_ge(z_cp, tt + 1)
                    o = ps[:, bank, tt // 2 * 256:(tt // 2 + 1) * 256]
                    mm(o, zmix[:, tt, g, 0, :], dft_c[:, tt, :], tt % 2 == 0, False)
                    ins = mm(o, zmix[:, tt, g, 1, :], dft_s[:, tt, :], False, tt % 2 == 1)
                ins.then_inc(four_mm, 1)

            def turn_qk(tt):
                pe.wait_ge(rot_done, tt + 1)
                if tt >= 2:
                    pe.wait_ge(qkT_cp, tt - 1)
                for i in range(5):
                    n = 8 * (tt % 2) + i
                    ins = nc.tensor.transpose(ps[:, 4 + n // 4, (n % 4) * P:(n % 4 + 1) * P],
                                              rot[:, tt, i * P:(i + 1) * P], ident)
                ins.then_inc(qkT_tr, 1)

            positions(0)
            turn_qk(0)
            turn_qk(1)
            positions(1)
            turn_qk(2)
            turn_qk(3)
            positions(2)
            pe.wait_ge(qkT_cp, NT)
            pe.wait_ge(four_cp, 2)

            def score(n):
                i, k = n // 8, n % 8
                hh, tt = k // NT, k % NT
                if n >= 2:
                    pe.wait_ge(p_done, n - 1)
                mm(ps[:, n % 2, :], qkT[64 * hh:64 * hh + 64, i, tt * P:(tt + 1) * P],
                   qkT[64 * hh:64 * hh + 64, 4, :], True, True).then_inc(s_mm, 1)

            def turn(n):
                pe.wait_ge(p_done, n + 1)
                if n >= 2:
                    pe.wait_ge(pT_cp, n - 1)
                for c in range(4):
                    ins = nc.tensor.transpose(ps[:, 2 + n % 2, c * P:(c + 1) * P], probs[:, n % 2, c * P:(c + 1) * P], ident)
                ins.then_inc(pT_tr, 1)

            def values(n):
                hh = n % 8 // NT
                pe.wait_ge(pT_cp, n + 1)
                if n >= 2:
                    pe.wait_ge(o_cp, n - 1)
                for c in range(4):
                    ins = mm(ps[:, 4 + n % 2, 0:64], probsT[:, n % 2, c, :], qkv[:, c, 640 + 64 * hh:704 + 64 * hh], c == 0, c == 3)
                ins.then_inc(o_mm, 1)

            units = 8 * PAIRS
            for n in range(units + 2):
                if n < units:
                    score(n)
                if n == 1:
                    positions(3)
                    pe.wait_ge(four_cp, 3)
                if 0 <= n - 1 < units:
                    turn(n - 1)
                if n >= 2:
                    values(n - 2)
            pe.wait_ge(four_cp, 4)

            def turn_heads(tt):
                pe.wait_ge(o_cp, units - NT + tt + 1)
                if tt >= 2:
                    pe.wait_ge(atT_cp, tt - 1)
                for i in range(4):
                    ins = nc.tensor.transpose(ps[:, 6 + tt % 2, i * P:(i + 1) * P], attn[:, tt, i * P:(i + 1) * P], ident)
                ins.then_inc(atT_tr, 1)

            def heads_ready(tt, hf, i):
                if i == 4 and tt == 0:
                    turn_heads(2 * hf)
                    turn_heads(2 * hf + 1)
                if i == 4 and hf == 0:
                    pe.wait_ge(atT_cp, tt + 1)

            arrived(IT_WOUT)
            arrived(IT_WOUT + 1)
            out_projection(0, IT_WOUT, heads_ready)
            moe(0)

            def v_half(n, tt):
                xT_ready(2, tt)
                if n == 1:
                    pe.wait_ge(v_pre, tt + 1)
                for j in range(NK):
                    ins = mm(ps[:, tt, :], xT[:, j, tt * P:(tt + 1) * P], owin(n)[:, j, :], j == 0, j == NK - 1)
                ins.then_inc(v_mm, 1)

            transpose_x(2, 0)
            arrived(IT_OWIN)
            for tt in range(NT):
                if tt < NT - 1:
                    transpose_x(2, tt + 1)
                v_half(0, tt)
            pe.wait_ge(small_in, 96)
            for hf in range(2):
                for g in range(4):
                    ins = nc.tensor.transpose(ps[:, 4 + hf, g * P:(g + 1) * P], ws[:, 4 * hf + g, :], ident)
                ins.then_inc(wsT_tr, 1)
            arrived(IT_OWIN + 1)
            for tt in range(NT):
                v_half(1, tt)
            pe.wait_ge(wsT_cp, 2)
            for n in range(8):
                if n % 4 == 0:
                    arrived(IT_OWIN + 2 + n // 4)
                if n >= 4:
                    pe.wait_ge(u_act, n - 3)
                for j in range(NK):
                    ins = mm(ps[:, 4 + n % 4, :], owin(2 + n // 4)[:, j, (n % 4) * P:(n % 4 + 1) * P], xT[:, j, :],
                             j == 0, j == NK - 1)
                ins.then_inc(u_mm, 1)
            pe.wait_ge(vln_done, NT)
            for g in range(CH):
                if g == 4:
                    pe.wait_ge(u_act, CH)
                for tt in range(NT):
                    ins = mm(ps[:, g, tt * P:(tt + 1) * P], vn[:, tt, g * P:(g + 1) * P], wsT[:, g, :], True, True)
                ins.then_inc(sp_mm, 1)
            arrived(IT_OWOUT)
            arrived(IT_OWOUT + 1)

            def gated_ready(tt, hf, i):
                if tt == 0 and hf == 0:
                    pe.wait_ge(uv_done, i + 1)

            out_projection(1, IT_OWOUT, gated_ready)
            moe(1)

        @block.scalar
        def _(act):
            norms = [None, ("ln_mix_g", "ln_mix_b", 0), ("ln_ffn_g", "ln_ffn_b", 0),
                     ("o_v_ln_g", "o_v_ln_b", 0), ("ln_mix_g", "ln_mix_b", 1), ("ln_ffn_g", "ln_ffn_b", 1)]

            def load_norm(k):
                for a in range(2):
                    act.dma_start(lnp[:, a, :], t[norms[k][a]][norms[k][2]].partition_broadcast(P)).then_inc(lnp_in, 16)

            act.dma_start(consts[:], t["consts"]).then_inc(const_in, 16)
            for a, name in enumerate(("e_q_gain", "e_k_gain")):
                act.dma_start(gains[:, a, :], t[name][0].partition_broadcast(P)).then_inc(small_in, 16)

            def root(k, tt):
                act.wait_ge(ln_stats, k * NT + tt + 1)
                nc.scalar.activation(std[:, tt:tt + 1], vare[:, tt:tt + 1], ACT.Sqrt).then_inc(ln_std, 1)

            def permute(r, tt):
                act.wait_ge(ln_done, r * NT + tt + 1)
                nc.scalar.activation(xperm[:, tt, :].rearrange("q (a j f) -> q a f j", a=4, j=NK),
                                     xres[:, tt, :].rearrange("q (a f j) -> q a f j", a=4, j=NK), ACT.Copy).then_inc(perm_done, 1)

            def copy_xT(r, tt):
                act.wait_ge(tr_done, r * 2 * NT + 2 * tt + 2)
                nc.scalar.activation(xT[:, 4:8, tt * P:(tt + 1) * P],
                                     ps[:, 4 + (2 * tt + 1) % 4, :].rearrange("p (k q) -> p k q", k=4), ACT.Copy)\
                    .then_inc(xT_act, 1)

            def norm_and_turn(r):
                for s in range(NT + 1):
                    if s < NT:
                        root(r, s)
                    if s >= 1:
                        copy_xT(r, s - 1)
                    if s < NT and r % 2:
                        permute(r, s)

            def moe(l):
                norm_and_turn(2 * l + 1)
                act.wait_ge(ln_done, (2 * l + 2) * NT)
                load_norm(2 if l == 0 else 5)
                act.wait_ge(lg_mm, l + 1)
                nc.scalar.activation(scores, ps[:, 0, 0:NT * E].rearrange("p (t e) -> p t e", t=NT), ACT.Sigmoid)\
                    .then_inc(sg_done, 1)
                for c in range(FC):
                    act.wait_ge(shg_mm, 4 * l + c + 1)
                    nc.scalar.activation(sh_sil[:, c, :], ps[:, 1 + c, :], ACT.Silu).then_inc(sh_silu, 1)
                act.wait_ge(shg_mm, 4 * (l + 1))
                act.dma_start(sh_down, t["sh_w_down"][l].rearrange("(p c) d -> p c d", c=FC)).then_inc(sh_down_in, 16)
                base = l * E

                def expert_step(n, u, first):
                    b = u % 2
                    act.wait_ge(gate_mm, n + (base + 1))
                    if not (first and u < 2):
                        act.wait_ge(h_done, n + (base - 1))
                    nc.scalar.activation(sil[:, b, :, :], ps[:, 2, 0:FC * NB].rearrange("p (c s) -> p c s", c=FC), ACT.Silu)\
                        .then_inc(silu_done, 1)
                    act.wait_ge(down_mm, n + (base + 1))
                    if not (first and u < 2):
                        act.wait_ge(scattered[b], (n - b) * 8 + 16 * (l * E // 2))
                    nc.scalar.activation(ysb[0:NB, b, 512:1024], ps[0:NB, 5, :], ACT.Copy,
                                         scale=w_slot[0:NB, bass.ds(n, 1)]).then_inc(y_act, 1)

                def quad(q, first):
                    act.wait_ge(idx_done, q + (l * QUADS + 1))
                    for u in range(SLOTS):
                        expert_step(q * SLOTS + u, u, first)

                quad(0, True)
                with act.Fori(1, QUADS - 1) as q:
                    quad(q, False)
                quad(QUADS - 1, False)
                overflow_act(act, l)
                act.wait_ge(acc_ready, l + 1)
                for tt in range(NT):
                    act.dma_start(xperm[:, tt, :], acc[l][tt * P:(tt + 1) * P, :]).then_inc(acc_in[tt], 16)

            norm_and_turn(0)
            act.wait_ge(ln_done, NT)
            load_norm(1)
            for g in range(4):
                if g == 1:
                    act.wait_ge(qk_ssq, 1)
                    nc.scalar.activation(qk_rs, qk_ss, ACT.Sqrt).then_inc(qk_root, 1)
                if g == 3:
                    for a in range(2):
                        act.wait_ge(fw_mm, 1)
                        nc.scalar.activation(fw[:, :, a, :], ps[:, 4 + a, :].rearrange("p (g d) -> p g d", g=4), ACT.Copy)\
                            .then_inc(fw_cp, 1)
                act.wait_ge(aT_mm, g + 1)
                nc.scalar.activation(aT[:, g, :], ps[:, g, :], ACT.Copy).then_inc(aT_cp, 1)
            for tt in range(NT):
                act.wait_ge(z_mm, tt + 1)
                nc.scalar.activation(zmix[:, tt, :, :, :].rearrange("p g s d -> p (g s d)"),
                                     ps[:, 6 - 2 * (tt % 2):8 - 2 * (tt % 2), :].rearrange("p b c -> p (b c)"), ACT.Copy)\
                    .then_inc(z_cp, 1)
            act.wait_ge(rot_done, NT)

            def copy_odd(g):
                act.wait_ge(four_mm, g + 1)
                if g == 3:
                    act.wait_ge(four_cp, 1)
                nc.scalar.activation(odd_sums[:, g % 3, :], ps[:, (0, 1, 3, 7)[g], 256:512], ACT.Copy).then_inc(odd_cp, 1)

            for g in range(3):
                copy_odd(g)

            def load_router(l):
                act.dma_start(router, t["router_w"][l].rearrange("(p j) e -> p j e", j=NK)).then_inc(router_in, 16)
                act.dma_start(rb_w, t["router_b"][l].partition_broadcast(P)).then_inc(router_in, 16)

            act.wait_ge(acc_out, 16 * DEPTH * (NT + 1))
            load_router(0)

            def exps(n, k, first):
                act.wait_ge(max_done, n + 1)
                if not (first and k < 2):
                    act.wait_ge(pT_tr, n - 1)
                if not (first and k < 4):
                    act.wait_ge(o_cp, n - 3)
                nc.scalar.activation(probs[:, k % 2, :], ps[:, k % 2, :], ACT.Exp, bias=nmax[:, k % 2:k % 2 + 1],
                                     accum_out=rsum[:, k % 4:k % 4 + 1]).then_inc(p_done, 1)

            def copy_pT(n, k, first):
                act.wait_ge(pT_tr, n + 1)
                if not (first and k < 2):
                    act.wait_ge(o_mm, n - 1)
                nc.scalar.activation(probsT[:, k % 2, :, :].rearrange("p c q -> p (c q)"), ps[:, 2 + k % 2, :], ACT.Copy)\
                    .then_inc(pT_cp, 1)

            act.wait_ge(z_cp, NT)
            for k in range(8):
                exps(k, k, True)
                if k == 1:
                    copy_odd(3)
                if k >= 1:
                    copy_pT(k - 1, k - 1, True)
            with act.Fori(1, PAIRS) as i:
                for k in range(8):
                    exps(i * 8 + k, k, False)
                    copy_pT(i * 8 + (k - 1), (k - 1) % 8, False)
            copy_pT(8 * PAIRS - 1, 7, False)
            moe(0)

            act.dma_start(ws, t["o_w_spatial"][0].rearrange("g p q -> p g q")).then_inc(small_in, 16)
            act.dma_start(bv_w, t["o_b_in"][0, D:2 * D].partition_broadcast(P)).then_inc(small_in, 16)
            act.dma_start(bs_w, t["o_b_spatial"][0].rearrange("g q -> (g q)").partition_broadcast(P)).then_inc(small_in, 16)
            act.dma_start(bu_col, t["u_bias"]).then_inc(small_in, 16)
            load_router(1)
            norm_and_turn(2)
            act.wait_ge(ln_done, 3 * NT)
            load_norm(3)

            def v_gelu(n):
                act.wait_ge(v_pre, n + 1)
                half = vn[:, n % NT, (n // NT) * 512:(n // NT + 1) * 512]
                nc.scalar.activation(half, half, ACT.Gelu).then_inc(v_act, 1)

            for tt in range(NT):
                v_gelu(tt)
            for hf in range(2):
                act.wait_ge(wsT_tr, hf + 1)
                nc.scalar.activation(wsT[:, 4 * hf:4 * hf + 4, :], ps[:, 4 + hf, :].rearrange("p (g q) -> p g q", g=4),
                                     ACT.Copy).then_inc(wsT_cp, 1)
            for tt in range(NT + 1):
                if tt < NT:
                    v_gelu(NT + tt)
                if tt >= 1:
                    act.wait_ge(vln_stats, tt)
                    nc.scalar.activation(std[:, tt - 1:tt], vare[:, tt - 1:tt], ACT.Sqrt).then_inc(vln_std, 1)
            act.wait_ge(small_in, 96)
            for n in range(8):
                act.wait_ge(u_mm, n + 1)
                nc.scalar.activation(uT[:, n, :], ps[:, 4 + n % 4, :], ACT.Gelu, bias=bu_col[:, n:n + 1]).then_inc(u_act, 1)
            act.wait_ge(vln_done, NT)
            load_norm(4)
            moe(1)
            for tt in range(NT):
                root(4, tt)

        @block.vector
        def _(dve):
            step = Steps(dve, dve_step)

            def norm_stats(src, tt, stats_sem):
                if step.n:
                    step.wait()
                for hf in range(2):
                    step.done(nc.vector.bn_stats(stats[:, tt, hf, :], src[:, tt, hf * 512:(hf + 1) * 512]))
                step.wait()
                step.done(nc.vector.bn_aggr(mv[:, tt, :], stats[:, tt, :, :].rearrange("p h s -> p (h s)")))
                step.wait()
                nc.vector.tensor_scalar(vare[:, tt:tt + 1], mv[:, tt, 1:2], LN_EPS, None, ALU.add).then_inc(stats_sem, 1)

            def norm_apply(src, tt, std_sem, std_value, order, done_sem):
                dve.wait_ge(std_sem, std_value)
                step.done(nc.vector.reciprocal(rstd[:, tt:tt + 1], std[:, tt:tt + 1]))
                dve.wait_ge(lnp_in, 32 * (order + 1))
                step.done(nc.vector.scalar_tensor_tensor(src[:, tt, :], src[:, tt, :], mv[:, tt, 0:1], lnp[:, 0, :],
                                                         ALU.subtract, ALU.mult))
                step.wait()
                nc.vector.scalar_tensor_tensor(src[:, tt, :], src[:, tt, :], rstd[:, tt:tt + 1], lnp[:, 1, :],
                                               ALU.mult, ALU.add).then_inc(done_sem, 1)

            def copy_xT(r, tt):
                dve.wait_ge(tr_done, r * 2 * NT + 2 * tt + 1)
                nc.vector.tensor_copy(xT[:, 0:4, tt * P:(tt + 1) * P],
                                      ps[:, 4 + 2 * tt % 4, :].rearrange("p (k q) -> p k q", k=4)).then_inc(xT_dve, 1)

            def norm(r, order, before_tile):
                for s in range(NT + 1):
                    if s < NT:
                        before_tile(s)
                        norm_stats(xres, s, ln_stats)
                    if s >= 1:
                        copy_xT(r, s - 1)
                    if s < NT:
                        norm_apply(xres, s, ln_std, r * NT + s + 1, order, ln_done)
                dve.wait_ge(ln_done, (r + 1) * NT)

            def add_projection(r):
                def tile(tt):
                    dve.wait_ge(wout_mm, r * NT + tt + 1)
                    nc.vector.scalar_tensor_tensor(xres[:, tt, :], xres[:, tt, :], ALPHA,
                                                   ps[:, 2 * (tt % 2):2 * (tt % 2) + 2, :].rearrange("p b c -> p (b c)"),
                                                   ALU.mult, ALU.add).then_inc(resid_done, 1)
                    dve.wait_ge(resid_done, r * NT + tt + 1)
                return tile

            def sum_ready(l):
                def tile(tt):
                    if tt == 0:
                        dve.wait_ge(acc_in[0], 16 * (l + 1))
                        nc.vector.tensor_tensor(xres[:, 0, :], xres[:, 0, :], xperm[:, 0, :], ALU.add).then_inc(first_sum, 1)
                        dve.wait_ge(first_sum, l + 1)
                    else:
                        dve.wait_ge(acc_sum, l * (NT - 1) + tt)
                return tile

            def bc(ap, shape):
                return ap.to_broadcast(shape)

            def moe(l):
                norm(1 + 2 * l, 1 if l == 0 else 4, add_projection(l))
                dve.wait_ge(bconst_in, 32)
                step.done(nc.vector.tensor_copy(tab[:, :, :, 0:3].rearrange("p t e c -> p t e c"),
                                                bc(posb.unsqueeze(2), [P, NT, E, 3])))
                dve.wait_ge(sg_done, l + 1)
                dve.wait_ge(router_in, 32 * (l + 1))
                step.done(nc.vector.tensor_tensor(sel, scores, bc(rb_w.unsqueeze(1), [P, NT, E]), ALU.add))
                step.wait()
                for tt in range(NT):
                    for g in range(N_EGROUPS):
                        step.done(nc.vector.max(m8[:, tt, g, :], sel[:, tt, g * 8:(g + 1) * 8]))
                step.wait()
                step.done(nc.vector.tensor_tensor(gsc, m8[:, :, :, 0], m8[:, :, :, 1], ALU.add))
                step.wait()
                mine, other = bc(gsc.unsqueeze(3), [P, NT, 8, 8]), bc(gsc.unsqueeze(2), [P, NT, 8, 8])
                step.done(nc.vector.tensor_tensor(cmps[0], other, mine, ALU.is_gt))
                step.done(nc.vector.tensor_tensor(cmps[1], other, mine, ALU.is_equal))
                step.wait()
                step.done(nc.vector.tensor_tensor(cmps[2], cmps[1], bc(earlier.unsqueeze(1), [P, NT, 8, 8]), ALU.mult))
                step.wait()
                step.done(nc.vector.tensor_tensor(cmps[1], cmps[0], cmps[2], ALU.add))
                step.wait()
                step.done(nc.vector.tensor_reduce(grank, cmps[1], AX, ALU.add))
                step.wait()
                step.done(nc.vector.tensor_scalar(gmask, grank, float(TOPK_GROUPS), None, ALU.is_lt))
                step.wait()
                step.done(nc.vector.tensor_scalar(gpen, gmask, BIG, BIG, ALU.mult, ALU.subtract))
                by_group = "p t (g k) -> p t g k"
                step.done(nc.vector.tensor_tensor(selm.rearrange(by_group, g=8), sel.rearrange(by_group, g=8),
                                                  bc(gmask.unsqueeze(3), [P, NT, 8, 8]), ALU.mult))
                step.wait()
                step.done(nc.vector.tensor_tensor(sel.rearrange(by_group, g=8), selm.rearrange(by_group, g=8),
                                                  bc(gpen.unsqueeze(3), [P, NT, 8, 8]), ALU.add))
                step.wait()
                for tt in range(NT):
                    step.done(nc.vector.max(v8[:, tt, :], sel[:, tt, :]))
                step.wait()
                for tt in range(NT):
                    step.done(nc.vector.match_replace(rep[:, tt, :], v8[:, tt, :], sel[:, tt, :], -3.0 * BIG))
                step.wait()
                nc.vector.tensor_scalar(maskb, rep, -2.0 * BIG, None, ALU.is_lt).then_inc(mask_done, 1)
                step.done(nc.vector.tensor_scalar(selm, rep, -2.0 * BIG, None, ALU.is_lt))
                step.wait()
                step.done(nc.vector.tensor_tensor(rep, scores, selm, ALU.mult))
                step.wait()
                step.done(nc.vector.tensor_reduce(wsum, rep, AX, ALU.add))
                step.wait()
                step.done(nc.vector.reciprocal(wfac, wsum))
                step.wait()
                step.done(nc.vector.tensor_scalar(wsum, wfac, ROUTE_SCALE, None, ALU.mult))
                step.wait()
                step.done(nc.vector.tensor_tensor(sel, rep, bc(wsum.unsqueeze(2), [P, NT, E]), ALU.mult))
                step.wait()
                step.done(nc.vector.tensor_copy(tab[:, :, :, 3], sel))
                step.wait()
                step.done(nc.vector.tensor_tensor(rep, sel, tab[:, :, :, 3], ALU.subtract))
                step.wait()
                step.done(nc.vector.tensor_copy(tab[:, :, :, 4], rep))
                step.wait()
                step.done(nc.vector.tensor_tensor(sel, rep, tab[:, :, :, 4], ALU.subtract))
                step.wait()
                nc.vector.tensor_copy(tab[:, :, :, 5], sel).then_inc(tab_done, 1)
                dve.wait_ge(rk_mm, l + 1)
                step.done(nc.vector.scalar_tensor_tensor(rep, ps[:, 5, 0:NT * E].rearrange("p (t e) -> p t e", t=NT), 1.0,
                                                         selm, ALU.add, ALU.mult))
                step.done(nc.vector.tensor_copy(cnt_tab, ps[:, 5, NT * E:(NT + 1) * E]))
                step.done(nc.vector.tensor_reduce(idx_f[:, 0:1], ps[:, 5, NT * E:(NT + 1) * E], AX, ALU.max))
                step.wait()
                nc.vector.tensor_copy(cnt_max, idx_f[:, 0:1]).then_inc(counts_ready, 1)
                step.done(nc.vector.tensor_scalar(rankm, rep, -1.0, None, ALU.add))
                step.wait()

                def choose(e, b, first, quads=0):
                    if not first:
                        dve.wait_ge(place_mm, quads + l * QUADS)
                    nc.vector.tensor_tensor(pick[:, b, :, :], bc(rankm[:, :, bass.ds(e, 1)], [P, NT, NB]),
                                            bc(iota.unsqueeze(1), [P, NT, NB]), ALU.is_equal).then_inc(pick_done, 1)

                def slot_table(q, first):
                    base = l * QUADS
                    dve.wait_ge(pick_mm, q * 4 + (l * E + 4))
                    dve.wait_ge(place_mm, q + (base + 1))
                    if not first:
                        dve.wait_ge(idx_done, q + base)
                    nc.vector.tensor_copy(pi_w[0:NB, 0:24], ps[0:NB, 7, 0:24])
                    nc.vector.tensor_tensor(place, ps[:, 7, 24:24 + 4 * NB].rearrange("p (a s) -> p a s", s=32),
                                            bc(mine32.unsqueeze(1), [P, 4 * BLOCKS, 32]), ALU.mult).then_inc(pi_cp, 1)
                    dve.wait_ge(pi_cp, q + (base + 1))
                    nc.vector.tensor_reduce(idx4_f, place, AX, ALU.add).then_inc(placed, 1)
                    v = pi[0:NB, :, :]
                    nc.vector.scalar_tensor_tensor(pi_idx[0:NB, :], v[:, :, 2], negslot[0:NB, :], v[:, :, 0],
                                                   ALU.mult, ALU.add)
                    nc.vector.tensor_tensor(pi_wt[0:NB, :], v[:, :, 3], v[:, :, 4], ALU.add).then_inc(pi_mid, 1)
                    dve.wait_ge(pi_mid, q + (base + 1))
                    dve.wait_ge(placed, q + (base + 1))
                    nc.vector.scalar_tensor_tensor(idx4_tab[:, bass.ds(q * 4 * BLOCKS, 4 * BLOCKS)], idx4_f, 4.0,
                                                   bc(quarter, [P, 4 * BLOCKS]), ALU.mult, ALU.add)
                    nc.vector.scalar_tensor_tensor(idx_tab[0:NB, bass.ds(q * 4, 4)], pi_idx[0:NB, :], dump[0:NB, :],
                                                   v[:, :, 1], ALU.add, ALU.add)
                    nc.vector.tensor_tensor(w_slot[0:NB, bass.ds(q * 4, 4)], pi_wt[0:NB, :], v[:, :, 5], ALU.add)\
                        .then_inc(idx_done, 1)

                def shared_mul(c):
                    dve.wait_ge(sh_silu, 2 * l + c + 1)
                    dve.wait_ge(shg_mm, 4 * l + 3 + c)
                    nc.vector.tensor_tensor(sh_h[:, c, :], sh_sil[:, c, :], ps[:, 4 + 2 * c, :], ALU.mult).then_inc(sh_mul, 1)

                for b in range(4):
                    choose(b, b, True)
                slot_table(0, True)
                shared_mul(0)
                for b in range(4):
                    choose(4 + b, b, False, 1)
                shared_mul(1)

                def add_shared(n):
                    dve.wait_ge(shd_mm, l * 2 * NT + n + 1)
                    half = xres[:, n // 2, (n % 2) * 512:(n % 2 + 1) * 512]
                    nc.vector.scalar_tensor_tensor(half, half, ALPHA, ps[:, 1 if n % 2 else 6, :], ALU.mult, ALU.add).then_inc(sh_y, 1)

                base = l * E

                def turn_tokens(n, u, b, first):
                    dve.wait_ge(gathered[u], (n - u) * 4 * BLOCKS + 16 * BLOCKS * (l * E // 4 + 1))
                    if not first:
                        dve.wait_ge(up_mm, n + (base - 1))
                    nc.vector.transpose(xgT[:, b, :, :].rearrange("p j (k s) -> p k j s", s=32),
                                        xg[:, u, :, :].rearrange("p k (j f) -> p k j f", f=32)).then_inc(xgT_done, 1)

                def expert_step(n, u, next_too, first, between):
                    b = u % 2
                    if next_too:
                        turn_tokens(n + 1, (u + 1) % SLOTS, 1 - b, first and u == 0)
                    between()
                    dve.wait_ge(silu_done, n + (base + 1))
                    dve.wait_ge(up_mm, n + (base + 1))
                    if not (first and u < 2):
                        dve.wait_ge(down_mm, n + (base - 1))
                    nc.vector.tensor_tensor(hT[:, b, :, :], sil[:, b, :, :],
                                            ps[:, 3, 0:FC * NB].rearrange("p (c s) -> p c s", c=FC), ALU.mult)\
                        .then_inc(h_done, 1)
                    dve.wait_ge(down_mm, n + (base + 1))
                    if not (first and u < 2):
                        dve.wait_ge(scattered[b], (n - b) * 8 + 16 * (l * E // 2))
                    nc.vector.tensor_scalar(ysb[0:NB, b, 0:512], ps[0:NB, 4, :], w_slot[0:NB, bass.ds(n, 1)], None, ALU.mult)\
                        .then_inc(y_dve, 1)

                def quad(q, first=False, shared=False, last=0):
                    for u in range(SLOTS):
                        def between():
                            if u == 0 and last < 2:
                                slot_table(q + 1, False)
                            if last < 1:
                                choose(q * 4 + (8 + u), u, False, q + 2)
                            if shared:
                                for k in SHARED.get(q * 4 + u, ()):
                                    add_shared(k)
                        expert_step(q * SLOTS + u, u, last < 2 or u < SLOTS - 1, first, between)

                turn_tokens(0, 0, 0, True)
                quad(0, first=True, shared=True)
                quad(1, shared=True)
                with dve.Fori(2, QUADS - 2) as q:
                    quad(q)
                quad(QUADS - 2, last=1)
                quad(QUADS - 1, last=2)
                overflow_dve(dve, step, l)
                dve.wait_ge(sh_y, 2 * NT * (l + 1))

            norm(0, 0, lambda tt: dve.wait_ge(x_in[tt], 16))
            dve.wait_ge(const_in, 16)
            dve.wait_ge(small_in, 32)
            step.done(nc.vector.tensor_scalar(gains[:, 0, :], gains[:, 0, :], HEAD_DIM ** -0.5, None, ALU.mult))
            for tt in range(NT):
                dve.wait_ge(qkv_mm, tt + 1)
                nc.vector.tensor_copy(qkv[:, tt, :], ps[:, 2 * tt:2 * tt + 2, :].rearrange("p b c -> p (b c)")[:, 0:QKV_WIDTH])\
                    .then_inc(qkv_cp, 1)
            for tt in range(NT):
                dve.wait_ge(qkv_cp, tt + 1)
                step.wait()
                step.done(nc.vector.tensor_tensor(tmp1, qkv[:, tt, 0:640], qkv[:, tt, 0:640], ALU.mult))
                step.wait()
                step.done(nc.vector.tensor_reduce(qk_rs[:, tt * 10:(tt + 1) * 10], tmp1.rearrange("p (h d) -> p h d", h=10),
                                                  AX, ALU.add))
            step.wait()
            nc.vector.tensor_scalar(qk_ss, qk_rs, 1.0 / HEAD_DIM, QK_EPS, ALU.mult, ALU.add).then_inc(qk_ssq, 1)
            dve.wait_ge(qk_root, 1)
            step.done(nc.vector.reciprocal(qk_ss, qk_rs))
            step.wait()
            for tt in range(NT):
                x = qkv[:, tt, 0:640]
                xh = x.rearrange("p (h d) -> p h d", h=10)
                step.done(nc.vector.tensor_tensor(tmp1.rearrange("p (h d) -> p h d", h=10), xh,
                                                  bc(qk_ss[:, tt * 10:(tt + 1) * 10].unsqueeze(2), [P, 10, 64]), ALU.mult))
                step.wait()
                for a, lo, hi in ((0, 0, 8), (1, 8, 10)):
                    step.done(nc.vector.tensor_tensor(xh[:, lo:hi, :], tmp1.rearrange("p (h d) -> p h d", h=10)[:, lo:hi, :],
                                                      bc(gains[:, a:a + 1, :], [P, hi - lo, 64]), ALU.mult))
                step.wait()
                step.done(nc.vector.tensor_tensor(tmp1.rearrange("p (h d) -> p h d", h=10), xh,
                                                  bc(rope_c[:, tt:tt + 1, :], [P, 10, 64]), ALU.mult))
                sv = rope_s[:, tt, :].rearrange("p (a r k) -> p a r k", a=2, r=2)
                for r in range(2):
                    for a in range(2):
                        step.done(nc.vector.tensor_tensor(
                            tmp2.rearrange("p (h a r k) -> p h a r k", h=10, a=2, r=2)[:, :, a, r, :],
                            x.rearrange("p (h a r k) -> p h a r k", h=10, a=2, r=2)[:, :, a, 1 - r, :],
                            bc(sv[:, a, r, :].unsqueeze(1), [P, 10, 16]), ALU.mult))
                step.wait()
                pair = "p (w i d) -> p w i d"
                step.done(nc.vector.tensor_tensor(rot[:, tt, 0:512].rearrange("p (i w d) -> p w i d", i=4, w=2),
                                                  tmp1[:, 0:512].rearrange(pair, w=2, i=4),
                                                  tmp2[:, 0:512].rearrange(pair, w=2, i=4), ALU.add))
                nc.vector.tensor_tensor(rot[:, tt, 512:640], tmp1[:, 512:640], tmp2[:, 512:640], ALU.add).then_inc(rot_done, 1)
                dve.wait_ge(rot_done, tt + 1)
                step.wait()

            def join_positions(g):
                dve.wait_ge(odd_cp, g + 1)
                even = ps[:, (0, 1, 3, 7)[g], 0:256]
                nc.vector.tensor_tensor(catT[:, g, 0:256], even, odd_sums[:, g % 3, :], ALU.add)
                nc.vector.tensor_tensor(catT[:, g, 256:512], even, odd_sums[:, g % 3, :], ALU.subtract).then_inc(four_cp, 1)

            def copy_qkT(tt):
                dve.wait_ge(qkT_tr, tt + 1)
                b0 = 4 + 2 * (tt % 2)
                nc.vector.tensor_copy(qkT[:, :, tt * P:(tt + 1) * P],
                                      ps[:, b0:b0 + 2, :].rearrange("p b c -> p (b c)")[:, 0:640]
                                      .rearrange("p (i q) -> p i q", i=5)).then_inc(qkT_cp, 1)

            for g in range(2):
                join_positions(g)
                for tt in (2 * g, 2 * g + 1):
                    copy_qkT(tt)
            join_positions(2)

            def row_max(n, k, first):
                dve.wait_ge(s_mm, n + 1)
                if not (first and k < 2):
                    dve.wait_ge(p_done, n - 1)
                nc.vector.tensor_reduce(nmax[:, k % 2:k % 2 + 1], ps[:, k % 2, :], AX, ALU.max, negate=True).then_inc(max_done, 1)

            def head_out(i, n, k, first):
                dve.wait_ge(p_done, n + 1)
                dve.wait_ge(o_mm, n + 1)
                hh, tt = k // NT, k % NT
                if not (first and k < 2):
                    dve.wait_ge(o_cp, n - 1)
                nc.vector.reciprocal(rinv[:, k % 2:k % 2 + 1], rsum[:, k % 4:k % 4 + 1]).then_inc(rinv_done, 1)
                dve.wait_ge(rinv_done, n + 1)
                nc.vector.tensor_scalar(attn[:, tt, bass.ds(i * 64 + 256 * hh, 64)], ps[:, 4 + k % 2, 0:64],
                                        rinv[:, k % 2:k % 2 + 1], None, ALU.mult).then_inc(o_cp, 1)

            for k in range(8):
                row_max(k, k, True)
                if k == 1:
                    join_positions(3)
                if k >= 2:
                    head_out(0, k - 2, k - 2, True)
            with dve.Fori(1, PAIRS) as i:
                for k in range(8):
                    row_max(i * 8 + k, k, False)
                    if k < 2:
                        head_out(i - 1, i * 8 + (k - 2), k + 6, False)
                    else:
                        head_out(i, i * 8 + (k - 2), k - 2, False)
            for k in (6, 7):
                head_out(PAIRS - 1, 8 * (PAIRS - 1) + k, k, False)
            for tt in range(NT):
                dve.wait_ge(atT_tr, tt + 1)
                nc.vector.tensor_copy(catT[:, 4:8, tt * P:(tt + 1) * P],
                                      ps[:, 6 + tt % 2, :].rearrange("p (i q) -> p i q", i=4)).then_inc(atT_cp, 1)
            moe(0)

            norm(2, 2, sum_ready(0))
            dve.wait_ge(small_in, 96)

            dve.wait_ge(counts_read, 1)

            def v_bias(n):
                dve.wait_ge(v_mm, n + 1)
                cols = slice((n // NT) * 512, (n // NT + 1) * 512)
                nc.vector.tensor_tensor(vn[:, n % NT, cols], ps[:, n % NT, :], bv_w[:, cols], ALU.add).then_inc(v_pre, 1)

            for tt in range(NT):
                v_bias(tt)
            for s in range(NT + 2):
                if s < NT:
                    v_bias(NT + s)
                if 1 <= s <= NT:
                    dve.wait_ge(v_act, NT + s)
                    norm_stats(vn, s - 1, vln_stats)
                if s >= 2:
                    norm_apply(vn, s - 2, vln_std, s - 1, 3, vln_done)
            dve.wait_ge(vln_done, NT)
            for g in range(CH):
                dve.wait_ge(u_act, g + 1)
                dve.wait_ge(sp_mm, g + 1)
                pv = ps[:, g, :].rearrange("p (n q) -> p n q", n=NT)
                tmpv = gate_tmp[:, g % 2, :]
                step.done(nc.vector.tensor_tensor(tmpv.rearrange("p (n q) -> p n q", n=NT), pv,
                                                  bc(bs[:, g:g + 1, :], [P, NT, P]), ALU.add))
                step.wait()
                nc.vector.tensor_tensor(uT[:, g, :], uT[:, g, :], tmpv, ALU.mult).then_inc(uv_done, 1)
                dve.wait_ge(uv_done, g + 1)
            moe(1)
            for s in range(NT + 1):
                if s < NT:
                    sum_ready(1)(s)
                    norm_stats(xres, s, ln_stats)
                if s >= 1:
                    norm_apply(xres, s - 1, ln_std, 4 * NT + s, 5, ln_done)

        @block.gpsimd
        def _(pool):
            step = Steps(pool, pool_step)

            def moe(l):
                for tt in range(NT):
                    pool.wait_ge(perm_done, l * NT + tt + 1)
                    pool.dma_start(xs[l][tt * P:(tt + 1) * P, :], xperm[:, tt, :]).then_inc(xs_out, 16)
                pool.wait_ge(xs_out, 64 * (l + 1))
                pool.wait_ge(counts_ready, l + 1)
                base = l * E

                def by_rows(n, steps, above, move):
                    count = pool.value_load(cnt_tab[0:1, bass.ds(n, 1)], min_val=0, max_val=T)

                    def choose(i):
                        if i == len(above):
                            move(steps[i])
                            return
                        with pool.If(count > above[i]):
                            move(steps[i])
                        with pool.Else():
                            choose(i + 1)
                        pool.nop()

                    choose(0)

                def gather(n, u, first, q):
                    if not first:
                        pool.wait_ge(scattered[u % 2], (n - u % 2) * 8 - 16 + 16 * (l * E // 2))
                        pool.wait_ge(xgT_done, n + (base - 3))
                    if u == 0:
                        pool.wait_ge(idx_done, q + (l * QUADS + 1))
                    pool.tensor_copy(idx_cur[0:NB, u:u + 1], idx_tab[0:NB, bass.ds(n, 1)])
                    pool.tensor_copy(idx4_cur[:, BLOCKS * u:BLOCKS * (u + 1)], idx4_tab[:, bass.ds(n * BLOCKS, BLOCKS)]).then_inc(idx_cp, 1)
                    pool.wait_ge(idx_cp, n + (base + 1))
                    pool.sem_inc(pool_tick, 1)

                    def block_in(k, rows):
                        pool.indirect_dma_start(
                            out=xg[0:rows, u, k, :], out_offset=None, in_=xs[l].rearrange("t (a c) -> (t a) c", a=4),
                            in_offset=bass.IndirectOffsetOnAxis(ap=idx4_cur[0:rows, BLOCKS * u + k:BLOCKS * u + k + 1], axis=0),
                            bounds_check=4 * T - 1, oob_is_err=False).then_inc(gathered[u], 16)

                    for k in range(BLOCKS - 1):
                        block_in(k, P)
                    by_rows(n, (P, 32), (NB - 32,), lambda rows: block_in(BLOCKS - 1, rows))

                def scatter(n, u, first):
                    b = u % 2
                    pool.wait_ge(y_dve, n + (base + 1))
                    pool.wait_ge(y_act, n + (base + 1))
                    if not (first and u == 0):
                        pool.wait_ge(scattered[1 - b], (n - u) * 8 + (16 * ((u + 1) // 2) + 16 * (l * E // 2)))
                    pool.sem_inc(pool_tick, 1)
                    by_rows(n, ROW_STEPS, ROW_STEPS[1:], lambda rows: pool.indirect_dma_start(
                        out=acc[l], out_offset=bass.IndirectOffsetOnAxis(ap=idx_cur[0:rows, u:u + 1], axis=0),
                        in_=ysb[0:rows, b, :], in_offset=None, bounds_check=T + NB - 1, oob_is_err=True,
                        compute_op=ALU.add).then_inc(scattered[b], 16))

                gather(0, 0, True, 0)
                gather(1, 1, True, 0)
                for u in range(SLOTS):
                    gather(u + 2, (u + 2) % SLOTS, u < 2, (u + 2) // SLOTS)
                    scatter(u, u, True)
                with pool.Fori(1, QUADS - 1) as i:
                    for u in range(SLOTS):
                        gather(i * SLOTS + (u + 2), (u + 2) % SLOTS, False, i + (u + 2) // SLOTS)
                        scatter(i * SLOTS + u, u, False)
                for u in range(SLOTS):
                    if u < 2:
                        gather(E - SLOTS + u + 2, u + 2, False, QUADS - 1)
                    scatter(E - SLOTS + u, u, False)
                for b in range(2):
                    pool.wait_ge(scattered[b], 16 * (l + 1) * E // 2)
                overflow_pool(pool, l)
                pool.sem_inc(acc_ready, 1)
                pool.wait_ge(sh_y, 2 * NT * (l + 1))
                for tt in range(1, NT):
                    pool.wait_ge(acc_in[tt], 16 * (l + 1))
                    pool.tensor_tensor(xres[:, tt, :], xres[:, tt, :], xperm[:, tt, :], ALU.add).then_inc(acc_sum, 1)

            pool.memset(zeros, 0.0).then_inc(zero_set, 1)
            pool.wait_ge(zero_set, 1)
            pool.wait_ge(qkv_mm, 1)
            for l in range(DEPTH):
                for lo in range(0, T + NB, P):
                    hi = min(lo + P, T + NB)
                    pool.dma_start(acc[l][lo:hi, :].rearrange("p (a c) -> p a c", a=8),
                                   zeros[0:hi - lo, :].unsqueeze(1).to_broadcast([hi - lo, 8, P])).then_inc(acc_out, 16)
            pool.dma_start(bconsts[:], t["bconsts"]).then_inc(bconst_in, 16)
            pool.dma_start(tok_all[:], t["tok_all"]).then_inc(bconst_in, 16)
            pool.wait_ge(acc_out, 16 * DEPTH * (NT + 1))
            moe(0)
            moe(1)


def tokens_by_parity():
    return np.concatenate([np.arange(0, T, 2), np.arange(1, T, 2)])


def constants():
    p = np.arange(P)
    c = np.zeros((P, 128 + 512 + 64 + NB + 2 + 33), np.float32)
    c[:, 0:128] = np.eye(P)
    pos = np.arange(T)
    inv = 10000.0 ** (-np.arange(16) / 16.0)
    ang = np.stack([pos // GRID_W, pos % GRID_W], -1)[:, :, None].astype(np.float32) * inv.astype(np.float32)
    cos, sin = np.cos(ang.astype(np.float64)), np.sin(ang.astype(np.float64))
    rc = np.stack([cos, cos], 2).reshape(T, 64)
    rs = np.stack([-sin, sin], 2).reshape(T, 64)
    c[:, 128:384] = rc.reshape(NT, P, 64).transpose(1, 0, 2).reshape(P, -1)
    c[:, 384:640] = rs.reshape(NT, P, 64).transpose(1, 0, 2).reshape(P, -1)
    c[:, 640:704] = (np.arange(8)[None, :] < np.arange(8)[:, None]).reshape(1, 64)
    c[:, 704:704 + NB] = np.arange(NB)
    c[:, 704 + NB] = -p
    c[:, 705 + NB] = T + p
    c[:, 706 + NB:738 + NB] = np.arange(32)[None, :] == p[:, None] % 32
    c[:, 738 + NB] = 4 * T + p // 32
    b = np.zeros((P, 256 + 12), np.float32)
    b[:, 0:128] = p[:, None] < p[None, :]
    b[:, 128:256] = 1
    for tt in range(NT):
        b[:, 256 + 3 * tt] = P * tt - T
        b[:, 257 + 3 * tt] = p
        b[:, 258 + 3 * tt] = 1
    tok = tokens_by_parity()
    a = 2 * np.pi * np.mod(np.outer(tok, np.arange(T // 2)), T) / T
    k = 2 * np.pi * np.mod(np.outer(p, p), P) / P
    d = np.zeros((P, 2304), np.float64)
    d[:, 0:1024] = np.cos(a).reshape(NT, P, T // 2).transpose(1, 0, 2).reshape(P, -1)
    d[:, 1024:2048] = np.sin(a).reshape(NT, P, T // 2).transpose(1, 0, 2).reshape(P, -1)
    d[:, 2048:2176] = np.cos(k) / math.sqrt(T * P)
    d[:, 2176:2304] = -np.sin(k) / math.sqrt(T * P)
    tok = np.arange(T).reshape(NT, P).T - T
    tok = np.broadcast_to(tok[:, :, None], (P, NT, P)).astype(np.float16)
    return {"consts": c, "bconsts": b, "dft": d.astype(np.float32), "tok_all": np.ascontiguousarray(tok)}


_INS = ["x", "ln_in_g", "ln_in_b", "e_w_in", "e_w_fourier", "e_q_gain", "e_k_gain", "e_w_out", "o_w_in", "o_b_in",
        "o_v_ln_g", "o_v_ln_b", "o_w_spatial", "o_b_spatial", "o_w_out", "ln_mix_g", "ln_mix_b", "ln_ffn_g", "ln_ffn_b",
        "router_w", "router_b", "exp_w_gate", "exp_w_up", "exp_w_down", "sh_w_gate", "sh_w_up", "sh_w_down"]


def kernel(**inputs):
    import concourse.bacc as _bacc
    from concourse.bass_utils import run_bass_kernel_spmd as _run

    nc = _bacc.Bacc("TRN2", target_bir_lowering=False, num_devices=1)
    arrays = {n: np.ascontiguousarray(inputs[n]) for n in _INS}
    arrays["u_bias"] = np.ascontiguousarray(arrays["o_b_in"][0, 0:D].reshape(CH, P).T)
    arrays.update(constants())
    t = {n: nc.dram_tensor(f"in_{n}", a.shape, mybir.dt.from_np(a.dtype), kind="ExternalInput").ap()
         for n, a in arrays.items()}
    out = nc.dram_tensor("out_x", [1, T, D], F32, kind="ExternalOutput").ap()
    build(nc, t, out)
    r = _run(nc, [{f"in_{n}": a for n, a in arrays.items()}], core_ids=[0])
    return r.results[0]["out_x"]
```
